# Optimizing a Trainium2 kernel written in Bass

```python
import math
import jax, jax.numpy as jnp
from jax import lax
import numpy as np

D_MODEL = 1024
BATCH = 1
SEQ = 256
DEPTH = 1

GRID_W = 64
WIN_H = 8
WIN_W = 16
NA_HEADS = 8
NA_HEAD_DIM = 64
NA_WIDTH = NA_HEADS * NA_HEAD_DIM
SG_GROUPS = 4
SG_GROUP_DIM = 128
SG_WIDTH = SG_GROUPS * SG_GROUP_DIM
SG_CHUNK = 128
IN_COLS = 3 * NA_WIDTH + 2 * SG_WIDTH + 2 * D_MODEL
PEER_HEADS = 8
PEER_N_KEYS = 128
PEER_N_EXPERTS = PEER_N_KEYS * PEER_N_KEYS
PEER_KEY_DIM = 256
PEER_HALF = PEER_KEY_DIM // 2
PEER_TOPK = 16
PEER_BLOCK = 128
DN_ALPHA = (2 * DEPTH) ** 0.25
DN_BETA = (8 * DEPTH) ** -0.25
LN_EPS = 1e-5

kernel_name = "hybrid_natten_sgu_peer_deepnorm"

def layer_norm(x, g, b):
    xf = x.astype(jnp.float32)
    mu = jnp.mean(xf, axis=-1, keepdims=True)
    xc = xf - mu
    var = jnp.mean(xc * xc, axis=-1, keepdims=True)
    y = xc * lax.rsqrt(var + LN_EPS)
    return (y * g.astype(jnp.float32) + b.astype(jnp.float32)).astype(x.dtype)

def neighbourhood_attention(q, k, v, rpb):
    b, s, h, dh = q.shape
    rows = s // GRID_W
    kh = min(WIN_H, rows)
    kw = WIN_W
    qg = q.reshape(b, rows, GRID_W, h, dh)
    kg = k.reshape(b, rows, GRID_W, h, dh)
    vg = v.reshape(b, rows, GRID_W, h, dh)
    cols = np.arange(GRID_W)
    col_start = np.clip(cols - kw // 2, 0, GRID_W - kw)
    col_idx = col_start[:, None] + np.arange(kw)[None, :]
    dc = col_idx - cols[:, None] + (WIN_W - 1)
    scale = dh ** -0.5

    def row_block(r):
        rs = jnp.clip(r - kh // 2, 0, rows - kh)
        q_r = lax.dynamic_index_in_dim(qg, r, axis=1, keepdims=False)
        k_r = lax.dynamic_slice_in_dim(kg, rs, kh, axis=1)[:, :, col_idx]
        v_r = lax.dynamic_slice_in_dim(vg, rs, kh, axis=1)[:, :, col_idx]
        dr = rs + jnp.arange(kh) - r + (WIN_H - 1)
        bias = rpb[:, dr[None, :, None], dc[:, None, :]]
        logits = jnp.einsum('bqhd,bkqwhd->bhqkw', q_r, k_r).astype(jnp.float32) * scale
        logits = logits + bias.astype(jnp.float32)[None]
        p = jax.nn.softmax(logits.reshape(b, h, GRID_W, kh * kw), axis=-1)
        p = p.reshape(b, h, GRID_W, kh, kw).astype(v.dtype)
        return jnp.einsum('bhqkw,bkqwhd->bqhd', p, v_r)

    out = lax.map(row_block, jnp.arange(rows))
    return out.transpose(1, 0, 2, 3, 4).reshape(b, s, h * dh)

def spatial_gating(u, v, norm_g, norm_b, w_s, b_s):
    b, s, _ = u.shape
    n = s // SG_CHUNK
    v = layer_norm(v, norm_g, norm_b)
    vc = v.reshape(b, n, SG_CHUNK, SG_GROUPS, SG_GROUP_DIM)
    mixed = jnp.einsum('gpq,bnqgc->bnpgc', w_s, vc) + b_s.T[None, None, :, :, None]
    return u * mixed.reshape(b, s, SG_WIDTH)

def peer_layer(x, wq, subkeys1, subkeys2, u_tab, v_tab):
    b, s, d = x.shape
    xb = x.reshape(b * s // PEER_BLOCK, PEER_BLOCK, d)

    def block(xt):
        q = (xt @ wq).reshape(PEER_BLOCK, PEER_HEADS, PEER_KEY_DIM)
        s1 = jnp.einsum('thd,nd->thn', q[..., :PEER_HALF], subkeys1).astype(jnp.float32)
        s2 = jnp.einsum('thd,nd->thn', q[..., PEER_HALF:], subkeys2).astype(jnp.float32)
        v1, i1 = lax.top_k(s1, PEER_TOPK)
        v2, i2 = lax.top_k(s2, PEER_TOPK)
        cand = (v1[..., :, None] + v2[..., None, :]).reshape(PEER_BLOCK, PEER_HEADS, PEER_TOPK * PEER_TOPK)
        vals, pos = lax.top_k(cand, PEER_TOPK)
        e1 = jnp.take_along_axis(i1, pos // PEER_TOPK, axis=-1)
        e2 = jnp.take_along_axis(i2, pos % PEER_TOPK, axis=-1)
        ids = e1 * PEER_N_KEYS + e2
        g = jax.nn.softmax(vals, axis=-1)
        a = jnp.einsum('td,thkd->thk', xt, u_tab[ids])
        hid = (jax.nn.gelu(a.astype(jnp.float32)) * g).astype(xt.dtype)
        return jnp.einsum('thk,thkd->td', hid, v_tab[ids])

    return lax.map(block, xb).reshape(b, s, d)

def setup_inputs(seed: int = 0) -> dict:
    key = jax.random.key(seed)
    ks = jax.random.split(key, 20)
    f32 = jnp.float32
    nrm = lambda k, shp, sc: jax.random.normal(k, shp, f32) * sc
    L = DEPTH
    return {
        "x": nrm(ks[0], (BATCH, SEQ, D_MODEL), 1.0),
        "w_in": nrm(ks[1], (L, D_MODEL, IN_COLS), D_MODEL ** -0.5),
        "na_rpb": nrm(ks[2], (L, NA_HEADS, 2 * WIN_H - 1, 2 * WIN_W - 1), 0.1),
        "sg_norm_g": 1.0 + nrm(ks[3], (L, SG_WIDTH), 0.02),
        "sg_norm_b": nrm(ks[4], (L, SG_WIDTH), 0.02),
        "sg_spatial_w": nrm(ks[5], (L, SG_GROUPS, SG_CHUNK, SG_CHUNK), SG_CHUNK ** -0.5),
        "sg_spatial_b": 1.0 + nrm(ks[6], (L, SG_GROUPS, SG_CHUNK), 0.02),
        "w_branch_na": nrm(ks[7], (L, NA_WIDTH, D_MODEL), NA_WIDTH ** -0.5),
        "w_branch_sg": nrm(ks[8], (L, SG_WIDTH, D_MODEL), SG_WIDTH ** -0.5),
        "w_out": nrm(ks[9], (L, D_MODEL, D_MODEL), DN_BETA * D_MODEL ** -0.5),
        "ln1_g": 1.0 + nrm(ks[10], (L, D_MODEL), 0.02),
        "ln1_b": nrm(ks[11], (L, D_MODEL), 0.02),
        "peer_wq": nrm(ks[12], (L, D_MODEL, PEER_HEADS * PEER_KEY_DIM), D_MODEL ** -0.5),
        "peer_subkeys1": nrm(ks[13], (L, PEER_N_KEYS, PEER_HALF), PEER_HALF ** -0.5),
        "peer_subkeys2": nrm(ks[14], (L, PEER_N_KEYS, PEER_HALF), PEER_HALF ** -0.5),
        "peer_u": nrm(ks[15], (L, PEER_N_EXPERTS, D_MODEL), D_MODEL ** -0.5),
        "peer_v": nrm(ks[16], (L, PEER_N_EXPERTS, D_MODEL), DN_BETA),
        "ln2_g": 1.0 + nrm(ks[17], (L, D_MODEL), 0.02),
        "ln2_b": nrm(ks[18], (L, D_MODEL), 0.02),
    }

def reference(x, w_in, na_rpb, sg_norm_g, sg_norm_b, sg_spatial_w, sg_spatial_b,
              w_branch_na, w_branch_sg, w_out, ln1_g, ln1_b, peer_wq, peer_subkeys1,
              peer_subkeys2, peer_u, peer_v, ln2_g, ln2_b):
    b, s, _ = x.shape
    splits = np.cumsum([NA_WIDTH, NA_WIDTH, NA_WIDTH, SG_WIDTH, SG_WIDTH, D_MODEL]).tolist()
    for l in range(DEPTH):
        proj = x @ w_in[l]
        q, k, v, su, sv, ga, gb = jnp.split(proj, splits, axis=-1)
        hd = (b, s, NA_HEADS, NA_HEAD_DIM)
        y_na = neighbourhood_attention(q.reshape(hd), k.reshape(hd), v.reshape(hd), na_rpb[l])
        y_sg = spatial_gating(jax.nn.gelu(su), jax.nn.gelu(sv), sg_norm_g[l], sg_norm_b[l],
                              sg_spatial_w[l], sg_spatial_b[l])
        merged = jax.nn.sigmoid(ga) * (y_na @ w_branch_na[l]) + jax.nn.sigmoid(gb) * (y_sg @ w_branch_sg[l])
        x = layer_norm(DN_ALPHA * x + merged @ w_out[l], ln1_g[l], ln1_b[l])
        y_peer = peer_layer(x, peer_wq[l], peer_subkeys1[l], peer_subkeys2[l], peer_u[l], peer_v[l])
        x = layer_norm(DN_ALPHA * x + y_peer, ln2_g[l], ln2_b[l])
    return x


_drawn_inputs = setup_inputs


def setup_inputs(seed=0):
    import zlib

    import numpy as np

    out = dict(_drawn_inputs(seed))
    spreads = {}
    factors = {'na_rpb': 2.869,
     'sg_norm_g': 3.716,
     'sg_norm_b': 3.712,
     'sg_spatial_b': 3.512,
     'ln2_g': 2.87,
     'ln2_b': 2.903}
    for name, (base, spread) in spreads.items():
        noise = np.random.default_rng([zlib.crc32(name.encode()), seed]).standard_normal(out[name].shape)
        drawn = base * np.exp(spread * noise) if base else spread * noise
        out[name] = __import__('jax').numpy.asarray(drawn.astype(out[name].dtype))
    for name, factor in factors.items():
        out[name] = (out[name] * factor).astype(out[name].dtype)
    return out
```

```python
import math

import concourse.bass as bass
from concourse import mybir

F32 = mybir.dt.float32
F32R = mybir.dt.float32r
U32 = mybir.dt.uint32
ALU = mybir.AluOpType
ACT = mybir.ActivationFunctionType
AX_X = mybir.AxisListType.X

P = 128
D = 1024
T = 256
TB = T // P
KD = D // P
HEADS, DH = 8, 64
GRID_W, ROWS = 64, T // 64
WIN_H, WIN_W = 8, 16
RPB_W = 2 * WIN_W - 1
RPB_H = 2 * WIN_H - 1
W5 = 512
KW = W5 // P
GROUPS = 4
PH = 8
NK = 128
TOPK = 16
SLOTS = PH * TOPK
NEXP = NK * NK
ALPHA = 2.0 ** 0.25
EPS = 1e-5
LOWEST = -3.0e38
MASKED = -1.0e30

CHUNKS = ["q", "k", "v", "ga0", "ga1", "gb0", "gb1", "sv", "su", "na", "sg", "o0", "o1", "w0", "w1", "w2", "w3"]
COL0 = {"q": 0, "k": W5, "v": 2 * W5, "su": 3 * W5, "sv": 4 * W5,
        "ga0": 5 * W5, "ga1": 6 * W5, "gb0": 7 * W5, "gb1": 8 * W5}
NHC = 2 * len(CHUNKS)
JOBS = []
for _c, _n in enumerate(CHUNKS):
    if _n in ("na", "sg"):
        JOBS += [(_n + "0", [2 * _c]), (_n + "1", [2 * _c + 1])]
    else:
        JOBS.append((_n, [2 * _c, 2 * _c + 1]))
JOB = {n: j for j, (n, _) in enumerate(JOBS)}
JOB_OF_HC = {h: j for j, (_, hs) in enumerate(JOBS) for h in hs}
LAST_HC = {j: hs[-1] for j, (_, hs) in enumerate(JOBS)}
HC = {n: 2 * c for c, n in enumerate(CHUNKS)}
ATT0 = HC["ga0"]


def free(ap, *dims, start=0):
    return bass.AP(ap.tensor, ap.offset + start, [list(ap.ap[0]), *[list(d) for d in dims]])


def hybrid_block(nc, x, w_in, na_rpb, sg_norm_g, sg_norm_b, sg_spatial_w, sg_spatial_b, w_branch_na,
                 w_branch_sg, w_out, ln1_g, ln1_b, peer_wq, peer_subkeys1, peer_subkeys2, peer_u,
                 peer_v, ln2_g, ln2_b, out):
    K1 = 1024
    base = 16512

    def sb(name, shape, at, dt=F32):
        return nc.alloc_sbuf_tensor_at(name, shape, dt, offset=base + int(at))

    ident = sb("ident", [P, P], 0)
    iota = sb("iota", [P, P], 512)
    act_hi = sb("act_hi", [P, KD, T], 1 * K1, F32R)
    act_lo = sb("act_lo", [P, KD, T], 9 * K1, F32R)
    xres = sb("xres", [P, TB, D], 17 * K1)
    w_raw = sb("w_raw", [P, 2, 2 * KW * W5], 25 * K1)
    w_hi = sb("w_hi", [P, 2, KW, W5], 57 * K1, F32R)
    w_lo = sb("w_lo", [P, 2, KW, W5], 73 * K1, F32R)
    qT = sb("qT", [P, KW, T], 89 * K1)
    kT = sb("kT", [P, KW, T], 93 * K1)
    v_sb = sb("v_sb", [P, TB, W5], 97 * K1)
    sv_sb = sb("sv_sb", [P, TB, W5], 101 * K1)
    su_sb = sb("su_sb", [P, TB, W5], 105 * K1)
    ysg = sb("ysg", [P, TB, W5], 109 * K1)
    ws_raw = sb("ws_raw", [P, GROUPS, P], 113 * K1)
    wsT = sb("wsT", [P, GROUPS, P], 115 * K1)
    sgn_g = sb("sgn_g", [P, W5], 117 * K1)
    sgn_b = sb("sgn_b", [P, W5], 119 * K1)
    bias = sb("bias", [P, HEADS, TB, T], 121 * K1)
    mrg_hi = sb("mrg_hi", [P, KD, T], 121 * K1, F32R)
    mrg_lo = sb("mrg_lo", [P, KD, T], 129 * K1, F32R)
    prob = sb("prob", [P, 2, TB, T], 137 * K1)
    probT = sb("probT", [P, 2, TB, T], 141 * K1)
    yna_hi = sb("yna_hi", [P, KW, T], 145 * K1, F32R)
    yna_lo = sb("yna_lo", [P, KW, T], 149 * K1, F32R)
    ysgT_hi = sb("ysgT_hi", [P, KW, T], 153 * K1, F32R)
    ysgT_lo = sb("ysgT_lo", [P, KW, T], 157 * K1, F32R)
    gates = sb("gates", [P, 2 * KD, T], 161 * K1)
    ln1g = sb("ln1g", [P, D], 177 * K1)
    ln1b = sb("ln1b", [P, D], 181 * K1)
    sk_raw = sb("sk_raw", [P, 2, P], 185 * K1)
    skT = sb("skT", [P, 2, P], 186 * K1)
    pqT = sb("pqT", [P, 2, KW, T], 89 * K1)
    sc = sb("sc", [P, PH, TB, 2, NK], 97 * K1)
    eq = sb("eq", [P, SLOTS, TOPK], 25 * K1)
    e1f = sb("e1f", [P, TB, SLOTS], 187 * K1)
    e2f = sb("e2f", [P, TB, SLOTS], 188 * K1)
    gw = sb("gw", [P, TB, SLOTS], 189 * K1)
    topv = sb("topv", [P, TB, PH, 2, TOPK], 190 * K1)
    topi = sb("topi", [P, TB, PH, 2, TOPK], 192 * K1, U32)
    topf = sb("topf", [P, TB, PH, 2, TOPK], 194 * K1)
    cand = sb("cand", [P, 2, TOPK * TOPK], 196 * K1)
    cand2 = sb("cand2", [P, TOPK * TOPK], 198 * K1)
    sc2 = sb("sc2", [P, NK], 199 * K1)
    cv = sb("cv", [P, TB, PH, TOPK], 200 * K1)
    cpos = sb("cpos", [P, TB, PH, TOPK], 201 * K1, U32)
    chalf = sb("chalf", [P, 2, TB, PH, TOPK], 202 * K1, U32)
    chalff = sb("chalff", [P, 2, TB, PH, TOPK], 204 * K1)
    G = sb("G", [P, NK * T], 25 * K1)
    onehot2 = sb("onehot2", [P, 8, NK], 193 * K1)
    onehot1g = sb("onehot1g", [P, 8, NK], 197 * K1)
    e1T = sb("e1T", [P, T], 189 * K1)
    e2T = sb("e2T", [P, T], 190 * K1)
    gT = sb("gT", [P, T], 191 * K1)
    u_raw = sb("u_raw", [P, 2, D], 153 * K1)
    v_raw = sb("v_raw", [P, 2, D], 161 * K1)
    uT_hi = sb("uT_hi", [P, 2, KD, P], 169 * K1, F32R)
    uT_lo = sb("uT_lo", [P, 2, KD, P], 177 * K1, F32R)
    v_hi = sb("v_hi", [P, 2, D], 185 * K1, F32R)
    v_lo = sb("v_lo", [P, 2, D], 193 * K1, F32R)
    act_e = sb("act_e", [P, 2, T], 201 * K1)
    hid_hi = sb("hid_hi", [P, 2, T], 203 * K1, F32R)
    hid_lo = sb("hid_lo", [P, 2, T], 205 * K1, F32R)
    ln2g = sb("ln2g", [P, D], 25 * K1)
    ln2b = sb("ln2b", [P, D], 29 * K1)
    small = sb("small", [P, 84], 207 * K1)
    stats = small[:, 0:24]
    mv = small[:, 24:28]
    rstd = small[:, 28:30]
    rmax = small[:, 32:36]
    rsum = small[:, 36:40]
    rinv = small[:, 40:44]
    eps = small[:, 44:45]
    bsT = small[:, 48:52]
    gsum = small[:, 52:68]
    ginv = small[:, 68:84]

    ps = nc.psum_tensor("ps", [P, 8, 512], F32).__enter__()

    def acc(j):
        return ps[:, 2 * (j % 2):2 * (j % 2) + 2, :].rearrange("p a b -> p (a b)")

    names = ["x_in", "rpb_in", "ws_in", "bs_in", "sgn_in", "ln1_in", "sk_in", "ln2_in",
             "w_in0", "w_in1", "w_hi_done", "w_lo_done", "w_used", "acc_free0", "acc_free1",
             "pool_done", "mask_done", "ident_ready", "tp_done", "tp_hi", "tp_lo", "tp_copied", "score_done", "logit_done",
             "max_done", "exp_done", "prob_ready", "probT_done", "probT_copied", "pv_done", "yna_hi_done",
             "yna_lo_done", "gelu_done", "mix_done", "sgln_done", "ysg_done", "ysgT_done", "ysgT_hi_done",
             "ysgT_lo_done", "merged_sum", "mrg_hi_done", "mrg_lo_done", "ln_var", "ln_std", "x1_ready",
             "act_hi_done", "act_lo_done", "key_scores", "sc_copied", "soft_in", "soft_exp", "route_done",
             "routeT_done", "routeT_copied", "onehots", "g_bank", "g_copied",
             "u_in0", "u_in1", "v_in0", "v_in1", "u_read", "uT_hi_done", "uT_lo_done", "v_hi_done",
             "v_lo_done", "a_done", "act_done", "hid_done", "hid_m", "hid_h", "y_done", "z_done", "out_ready",
             "stored", "dve"]
    s = {n: nc.semaphore(n).__enter__() for n in names}

    class Chain:

        def __init__(self, eng, sem):
            self.eng, self.sem, self.n = eng, sem, 0

        def step(self, ins):
            ins.then_inc(self.sem, 1)
            self.n += 1
            return self.n

        def wait(self, n=None):
            self.eng.wait_ge(self.sem, self.n if n is None else n)

    u_dram = peer_u[0]
    v_dram = peer_v[0]

    def chunk_source(n):
        if n in COL0:
            return w_in[0, :, COL0[n]:COL0[n] + W5].rearrange("(k p) n -> p k n", p=P)
        if n in ("na", "sg"):
            w = w_branch_na if n == "na" else w_branch_sg
            return w[0].rearrange("(k p) n -> p k n", p=P)
        w = w_out if n[0] == "o" else peer_wq
        c = int(n[1]) * W5
        return w[0, :, c:c + W5].rearrange("(k p) n -> p k n", p=P)

    def half_source(hc):
        c = hc // 2
        raw = w_raw[:, c % 2, :]
        if CHUNKS[c] in ("na", "sg"):
            return raw.rearrange("p (k n) -> p k n", k=KW)[:, :, (hc % 2) * W5:(hc % 2 + 1) * W5]
        return raw.rearrange("p (k n) -> p k n", k=KD)[:, (hc % 2) * KW:(hc % 2 + 1) * KW, :]

    NB = NK

    blocks = nc.Block()
    block = blocks.__enter__()

    @block.sync
    def _(sp):
        sp.dma_start(xres[:], x[0].rearrange("(b p) d -> p b d", p=P)).then_inc(s["x_in"], 16)
        for c, n in enumerate(CHUNKS):
            if c >= 2:
                sp.wait_ge(s["w_lo_done"], 2 * (c - 1))
            k = KW if n in ("na", "sg") else KD
            sp.dma_start(w_raw[:, c % 2, :].rearrange("p (k n) -> p k n", k=k), chunk_source(n)) \
                .then_inc(s[f"w_in{c % 2}"], 16)
            if c == 0:
                sp.dma_start(ws_raw[:], sg_spatial_w[0].rearrange("g p q -> p g q")).then_inc(s["ws_in"], 16)
                sp.dma_start(sk_raw[:, 0, :], peer_subkeys1[0]).then_inc(s["sk_in"], 16)
                sp.dma_start(sk_raw[:, 1, :], peer_subkeys2[0]).then_inc(s["sk_in"], 16)
            if c == 1:
                for h in range(HEADS):
                    for r in range(ROWS):
                        at = (h * RPB_H + WIN_H - ROWS + r) * RPB_W + WIN_W - GRID_W
                        src = bass.AP(na_rpb.tensor, na_rpb.offset + at,
                                      [[1, GRID_W], [RPB_W, ROWS], [1, GRID_W]])
                        b, p0 = r // 2, GRID_W * (r % 2)
                        dst = bias[p0:p0 + GRID_W, h, b, :].rearrange("p (r c) -> p r c", r=ROWS)
                        sp.dma_start(dst, src).then_inc(s["rpb_in"], 16)
                sp.dma_start(bsT, sg_spatial_b[0].rearrange("g p -> p g"),
                             allow_slow_non_contiguous=True).then_inc(s["bs_in"], 16)
                sp.dma_start(sgn_g[:], sg_norm_g[0:1, :].broadcast_to([P, W5])).then_inc(s["sgn_in"], 16)
                sp.dma_start(sgn_b[:], sg_norm_b[0:1, :].broadcast_to([P, W5])).then_inc(s["sgn_in"], 16)
                sp.dma_start(ln1g[:], ln1_g[0:1, :].broadcast_to([P, D])).then_inc(s["ln1_in"], 16)
                sp.dma_start(ln1b[:], ln1_b[0:1, :].broadcast_to([P, D])).then_inc(s["ln1_in"], 16)

        def load_block(b, slot):
            sp.dma_start(u_raw[:, slot, :], u_dram[bass.ds(b * P, P), :]).then_inc(s[f"u_in{slot}"], 16)
            sp.dma_start(v_raw[:, slot, :], v_dram[bass.ds(b * P, P), :]).then_inc(s[f"v_in{slot}"], 16)

        sp.wait_ge(s["mrg_lo_done"], 2)
        load_block(0, 0)
        load_block(1, 1)
        with sp.Fori(1, NB // 2) as i:
            for slot in range(2):
                sp.wait_ge(s["u_read"], 2 * i + slot - 1)
                sp.dma_start(u_raw[:, slot, :], u_dram[bass.ds((2 * i + slot) * P, P), :]) \
                    .then_inc(s[f"u_in{slot}"], 16)
                sp.wait_ge(s["v_lo_done"], 2 * i + slot - 1)
                sp.dma_start(v_raw[:, slot, :], v_dram[bass.ds((2 * i + slot) * P, P), :]) \
                    .then_inc(s[f"v_in{slot}"], 16)
        sp.wait_ge(s["hid_m"], NB)
        sp.dma_start(ln2g[:], ln2_g[0:1, :].broadcast_to([P, D])).then_inc(s["ln2_in"], 16)
        sp.dma_start(ln2b[:], ln2_b[0:1, :].broadcast_to([P, D])).then_inc(s["ln2_in"], 16)
        for b in range(TB):
            sp.wait_ge(s["out_ready"], b + 1)
            sp.dma_start(out[0, b * P:(b + 1) * P, :], xres[:, b, :]).then_inc(s["stored"], 16)
        sp.wait_ge(s["stored"], 16 * TB)

    @block.gpsimd
    def _(pool):
        pool.memset(ident[:], 0.0).then_inc(s["pool_done"], 1)
        pool.wait_ge(s["pool_done"], 1)
        pool.affine_select(out=ident[:], in_=ident[:], compare_op=ALU.not_equal, fill=1.0, base=0,
                           pattern=[[-1, P]], channel_multiplier=1).then_inc(s["ident_ready"], 1)
        pool.wait_ge(s["ident_ready"], 1)
        pool.iota(iota[:], [[1, P]], base=0, channel_multiplier=0,
                  allow_small_or_imprecise_dtypes=True).then_inc(s["ident_ready"], 1)
        pool.wait_ge(s["ident_ready"], 2)
        pool.memset(eps, EPS).then_inc(s["ident_ready"], 1)
        pool.wait_ge(s["ident_ready"], 3)
        pool.wait_ge(s["rpb_in"], 16 * ROWS * HEADS)
        rows = HEADS * TB * ROWS
        for n, p0 in enumerate((0, GRID_W)):
            if n:
                pool.wait_ge(s["mask_done"], 1)
            both = bias[p0:p0 + GRID_W].rearrange("p h b (r c) -> p (h b r) c", c=GRID_W)
            low = both[:, :, WIN_W:GRID_W]
            pool.affine_select(out=low, in_=low, compare_op=ALU.is_ge, fill=MASKED,
                               base=GRID_W - 1 - WIN_W + WIN_W // 2,
                               pattern=[[0, rows], [-1, GRID_W - WIN_W]],
                               channel_multiplier=-1).then_inc(s["mask_done"], 1)
        for n, p0 in enumerate((0, GRID_W)):
            both = bias[p0:p0 + GRID_W].rearrange("p h b (r c) -> p (h b r) c", c=GRID_W)
            high = both[:, :, 0:GRID_W - WIN_W]
            pool.wait_ge(s["mask_done"], n + 2)
            pool.affine_select(out=high, in_=high, compare_op=ALU.is_ge, fill=MASKED,
                               base=WIN_W // 2 - GRID_W,
                               pattern=[[0, rows], [1, GRID_W - WIN_W]],
                               channel_multiplier=1).then_inc(s["mask_done"], 1)

    @block.scalar
    def _(act):
        def split_act(n, first_tp):
            for g in range(4):
                act.wait_ge(s["tp_done"], first_tp + g + 1)
                act.activation(act_hi[:, 2 * g:2 * g + 2, :].rearrange("p a b -> p (a b)"), ps[:, 4 + g, :],
                               ACT.Copy).then_inc(s["act_hi_done"], 1)

        split_act(0, 0)
        act.wait_ge(s["tp_done"], 5)
        act.activation(wsT[:].rearrange("p a b -> p (a b)"), ps[:, 4, :], ACT.Copy).then_inc(s["tp_copied"], 1)
        act.wait_ge(s["tp_done"], 6)
        act.activation(skT[:].rearrange("p a b -> p (a b)"), ps[:, 5, 0:2 * P], ACT.Copy) \
            .then_inc(s["tp_copied"], 1)

        def free_acc(ins, j):
            ins.then_inc(s[f"acc_free{j % 2}"], 1)

        def evacuate(j):
            name = JOBS[j][0]
            a = acc(j)
            act.wait_ge(s["w_used"], LAST_HC[j] + 1)
            if name in ("q", "k", "v"):
                dst = {"q": qT, "k": kT, "v": v_sb}[name]
                free_acc(act.activation(dst[:].rearrange("p a b -> p (a b)"), a, ACT.Copy), j)
            elif name[0] == "g":
                i = j - JOB["ga0"]
                dst = gates[:, 4 * i:4 * i + 4, :].rearrange("p a b -> p (a b)")
                free_acc(act.activation(dst, a, ACT.Tanh, scale=0.5), j)
            elif name in ("sv", "su"):
                dst = sv_sb if name == "sv" else su_sb
                free_acc(act.activation(dst[:].rearrange("p a b -> p (a b)"), a, ACT.Gelu_apprx_tanh), j)
            elif name in ("w0", "w1", "w2", "w3"):
                i = int(name[1])
                if i >= 2:
                    act.wait_ge(s["key_scores"], i - 1)
                free_acc(act.activation(pqT[:, i % 2].rearrange("p a b -> p (a b)"), a, ACT.Copy), j)

        def attention_exp(h):
            act.wait_ge(s["max_done"], h + 1)
            for b in range(TB):
                act.activation(prob[:, h % 2, b, :], prob[:, h % 2, b, :], ACT.Exp,
                               bias=rmax[:, 2 * (h % 2) + b:2 * (h % 2) + b + 1],
                               accum_out=rsum[:, 2 * (h % 2) + b:2 * (h % 2) + b + 1]).then_inc(s["exp_done"], 1)

        def copy_probT(h):
            act.wait_ge(s["probT_done"], h + 1)
            if h >= 2:
                act.wait_ge(s["pv_done"], h - 1)
            act.activation(probT[:, h % 2].rearrange("p a b -> p (a b)"), ps[:, 5, :], ACT.Copy) \
                .then_inc(s["probT_copied"], 1)

        def yna_split(pair):
            act.wait_ge(s["pv_done"], 2 * pair + 2)
            act.activation(yna_hi[:, pair, :], ps[:, 6, 0:T], ACT.Copy).then_inc(s["yna_hi_done"], 1)

        def ysg_split():
            for b in range(2):
                act.wait_ge(s["ysgT_done"], b + 1)
                act.activation(ysgT_hi[:, 2 * b:2 * b + 2, :].rearrange("p a b -> p (a b)"), ps[:, 4 + b, :],
                               ACT.Copy).then_inc(s["ysgT_hi_done"], 1)

        def sqrt_var(n, cols):
            act.wait_ge(s["ln_var"], TB * (n + 1))
            act.activation(rstd[:, 0:cols], mv.rearrange("p (b s) -> p b s", s=2)[:, 0:cols, 1], ACT.Sqrt,
                           bias=eps).then_inc(s["ln_std"], 1)

        def copy_scores(i):
            act.wait_ge(s["key_scores"], i + 1)
            act.activation(sc[:, 2 * i:2 * i + 2].rearrange("p a b c d -> p (a b c d)"),
                           ps[:, 4:6, :].rearrange("p a b -> p (a b)"), ACT.Copy).then_inc(s["sc_copied"], 1)

        for hc in range(NHC + 2):
            if hc < NHC:
                c = hc // 2
                act.wait_ge(s[f"w_in{c % 2}"], 16 * (c // 2 + 1))
                if hc >= 2:
                    act.wait_ge(s["w_used"], hc - 1)
                act.activation(w_hi[:, hc % 2], half_source(hc), ACT.Copy).then_inc(s["w_hi_done"], 1)
            for j in range(len(JOBS)):
                if LAST_HC[j] == hc - 1 and not JOBS[j][0].startswith(("na", "sg", "o")):
                    evacuate(j)
            h = hc - ATT0 - 1
            if 0 <= h < HEADS:
                attention_exp(h)
            if 0 <= h - 2 < HEADS:
                copy_probT(h - 2)
            if h - 4 >= 1 and (h - 4) % 2 == 1 and h - 4 < HEADS:
                yna_split((h - 4) // 2)
            if hc == HC["sv"] + 2:
                sqrt_var(0, TB)
            if hc == HC["sg"]:
                ysg_split()
            if hc in (HC["sg"] + 1, HC["sg"] + 2):
                i = hc - HC["sg"] - 1
                act.wait_ge(s["merged_sum"], i + 1)
                act.activation(mrg_hi[:, 4 * i:4 * i + 4, :].rearrange("p a b -> p (a b)"),
                               gates[:, 4 * i:4 * i + 4, :].rearrange("p a b -> p (a b)"), ACT.Copy,
                               scale=0.5).then_inc(s["mrg_hi_done"], 1)
            if hc == HC["w0"]:
                sqrt_var(1, TB)
                split_act(1, 6)
            if HC["w0"] + 3 <= hc and (hc - HC["w0"] - 3) % 2 == 0 and (hc - HC["w0"] - 3) // 2 < 4:
                copy_scores((hc - HC["w0"] - 3) // 2)
        act.wait_ge(s["soft_in"], 1)
        act.activation(gw[:].rearrange("p a b -> p (a b)"), gw[:].rearrange("p a b -> p (a b)"), ACT.Exp) \
            .then_inc(s["soft_exp"], 1)
        act.wait_ge(s["routeT_done"], 1)
        for n, dst in enumerate((e1T, e2T, gT)):
            act.activation(dst[:], ps[:, 4 + n, 0:T], ACT.Copy).then_inc(s["routeT_copied"], 1)
        G3 = G[:].rearrange("p (e t) -> p e t", t=T)
        with act.Fori(0, T // 8) as i:
            for half in range(2):
                act.wait_ge(s["g_bank"], 2 * i + half + 1)
                act.activation(G3[:, :, bass.ds(8 * i + 4 * half, 4)],
                               ps[:, half, :].rearrange("p (t e) -> p e t", t=4), ACT.Copy) \
                    .then_inc(s["g_copied"], 1)

        def split_uT(b, slot):
            act.wait_ge(s["u_read"], b + 1)
            act.activation(uT_hi[:, slot].rearrange("p a b -> p (a b)"),
                           ps[:, 6:8, :].rearrange("p a b -> p (a b)"), ACT.Copy).then_inc(s["uT_hi_done"], 1)

        def pair(i, head, tail):
            for slot in range(2):
                b = 2 * i + slot
                act.wait_ge(s["a_done"], b + 1)
                if not (head and slot < 2):
                    act.wait_ge(s["hid_done"], b - 1)
                act.activation(act_e[:, slot, :], ps[:, 4 + slot, 0:T], ACT.Gelu_apprx_tanh) \
                    .then_inc(s["act_done"], 1)
                if tail and slot == 1:
                    continue
                split_uT(b + 1, 1 - slot)
                if not (head and slot == 0):
                    act.wait_ge(s["y_done"], b)
                act.wait_ge(s[f"v_in{1 - slot}"], 16 * (i + 1) if slot == 0 else 16 * i + 32)
                act.activation(v_hi[:, 1 - slot, :], v_raw[:, 1 - slot, :], ACT.Copy).then_inc(s["v_hi_done"], 1)

        split_uT(0, 0)
        act.wait_ge(s["v_in0"], 16)
        act.activation(v_hi[:, 0, :], v_raw[:, 0, :], ACT.Copy).then_inc(s["v_hi_done"], 1)
        pair(0, True, False)
        with act.Fori(1, NB // 2 - 1) as i:
            pair(i, False, False)
        pair(NB // 2 - 1, False, True)
        sqrt_var(2, TB)

    @block.vector
    def _(dve):
        ch = Chain(dve, s["dve"])

        def split_act(first_tp, first_hi):
            for g in range(4):
                dve.wait_ge(s["act_hi_done"], first_hi + g + 1)
                dst = act_lo[:, 2 * g:2 * g + 2, :].rearrange("p a b -> p (a b)")
                hi = act_hi[:, 2 * g:2 * g + 2, :].rearrange("p a b -> p (a b)").bitcast(F32)
                dve.tensor_tensor(dst, ps[:, 4 + g, :], hi, ALU.subtract).then_inc(s["act_lo_done"], 1)

        def layer_norm(n, src, width, g, b, dst, done, gb_in, blocks=TB):
            parts = width // 512
            ch.wait()
            for t in range(blocks):
                for q in range(parts):
                    ch.step(dve.bn_stats(stats[:, 12 * t + 6 * q:12 * t + 6 * q + 6],
                                         src[:, t, 512 * q:512 * q + 512]))
            for t in range(blocks):
                ch.wait()
                dve.bn_aggr(mv[:, 2 * t:2 * t + 2], stats[:, 12 * t:12 * t + 6 * parts]) \
                    .then_inc(s["ln_var"], 1)
            dve.wait_ge(s["ln_std"], n + 1)
            ch.step(dve.reciprocal(rstd[:, 0:2], rstd[:, 0:2]))
            ch.wait()
            dve.wait_ge(gb_in, 32)
            for t in range(blocks):
                ch.step(dve.tensor_scalar(dst[:, t, :], src[:, t, :], mv[:, 2 * t:2 * t + 1],
                                          rstd[:, t:t + 1], ALU.subtract, ALU.mult))
                ch.wait()
                ch.step(dve.tensor_tensor(dst[:, t, :], dst[:, t, :], g[:], ALU.mult))
                ch.wait()
                dve.tensor_tensor(dst[:, t, :], dst[:, t, :], b[:], ALU.add).then_inc(done, 1)

        split_act(0, 0)

        def logits(h):
            dve.wait_ge(s["score_done"], h + 1)
            dve.wait_ge(s["mask_done"], 4)
            if h >= 2:
                dve.wait_ge(s["probT_done"], h - 1)
            dve.scalar_tensor_tensor(prob[:, h % 2], ps[:, 4, :].rearrange("p (b k) -> p b k", b=TB), DH ** -0.5,
                                     free(bias[:, h, 0, :], (T, TB), (-1, T), start=T - 1),
                                     ALU.mult, ALU.add).then_inc(s["logit_done"], 1)
            dve.wait_ge(s["logit_done"], h + 1)
            m = rmax[:, 2 * (h % 2):2 * (h % 2) + 2]
            ch.step(dve.tensor_reduce(m, prob[:, h % 2], AX_X, ALU.max))
            ch.wait()
            dve.tensor_scalar(m, m, -1.0, None, ALU.mult).then_inc(s["max_done"], 1)

        def normalise(h):
            dve.wait_ge(s["exp_done"], 2 * h + 2)
            r = rinv[:, 2 * (h % 2):2 * (h % 2) + 2]
            ch.step(dve.reciprocal(r, rsum[:, 2 * (h % 2):2 * (h % 2) + 2]))
            ch.wait()
            for b in range(TB):
                dve.tensor_scalar(prob[:, h % 2, b, :], prob[:, h % 2, b, :], r[:, b:b + 1], None,
                                  ALU.mult).then_inc(s["prob_ready"], 1)

        def yna_split(pair):
            dve.wait_ge(s["yna_hi_done"], pair + 1)
            dve.tensor_tensor(yna_lo[:, pair, :], ps[:, 6, 0:T], yna_hi[:, pair, :].bitcast(F32),
                              ALU.subtract).then_inc(s["yna_lo_done"], 1)

        def gate_spatial():
            dve.wait_ge(s["bs_in"], 16)
            dve.wait_ge(s["acc_free%d" % (JOB["su"] % 2)], JOB["su"] // 2 + 1)
            for b in range(TB):
                dve.wait_ge(s["mix_done"], b + 1)
                for g in range(GROUPS):
                    dve.scalar_tensor_tensor(ysg[:, b, g * P:(g + 1) * P], ps[:, 6 + b, g * P:(g + 1) * P],
                                             bsT[:, g:g + 1], su_sb[:, b, g * P:(g + 1) * P],
                                             ALU.add, ALU.mult).then_inc(s["ysg_done"], 1)

        def ysg_split():
            for b in range(2):
                dve.wait_ge(s["ysgT_hi_done"], b + 1)
                hi = ysgT_hi[:, 2 * b:2 * b + 2, :].rearrange("p a b -> p (a b)").bitcast(F32)
                dve.tensor_tensor(ysgT_lo[:, 2 * b:2 * b + 2, :].rearrange("p a b -> p (a b)"),
                                  ps[:, 4 + b, :], hi, ALU.subtract).then_inc(s["ysgT_lo_done"], 1)

        def merge(j):
            name = JOBS[j][0]
            dve.wait_ge(s["w_used"], LAST_HC[j] + 1)
            i = int(name[-1])
            ga = gates[:, 4 * i:4 * i + 4, :].rearrange("p a b -> p (a b)")
            gb = gates[:, 8 + 4 * i:12 + 4 * i, :].rearrange("p a b -> p (a b)")
            if name[:2] == "na":
                dve.wait_ge(s[f"acc_free{(JOB['gb1']) % 2}"], JOB["gb1"] // 2 + 1)
                dve.wait_ge(s[f"acc_free{(JOB['gb0']) % 2}"], JOB["gb0"] // 2 + 1)
                ins = dve.scalar_tensor_tensor(ga, ga, 1.0, acc(j), ALU.add, ALU.mult)
                ins.then_inc(s[f"acc_free{j % 2}"], 1)
            else:
                dve.scalar_tensor_tensor(gb, gb, 1.0, acc(j), ALU.add, ALU.mult) \
                    .then_inc(s[f"acc_free{j % 2}"], 1)
                dve.wait_ge(s[f"acc_free{j % 2}"], j // 2 + 1)
                dve.tensor_tensor(ga, ga, gb, ALU.add).then_inc(s["merged_sum"], 1)
                dve.wait_ge(s["mrg_hi_done"], i + 1)
                hi = mrg_hi[:, 4 * i:4 * i + 4, :].rearrange("p a b -> p (a b)").bitcast(F32)
                dve.scalar_tensor_tensor(mrg_lo[:, 4 * i:4 * i + 4, :].rearrange("p a b -> p (a b)"),
                                         ga, 0.5, hi, ALU.mult, ALU.subtract).then_inc(s["mrg_lo_done"], 1)

        def residual(i):
            j = JOB["o0"] + i
            dve.wait_ge(s["w_used"], LAST_HC[j] + 1)
            cols = xres[:, :, i * W5:(i + 1) * W5]
            dve.scalar_tensor_tensor(cols, cols, ALPHA, acc(j).rearrange("p (b n) -> p b n", b=TB),
                                     ALU.mult, ALU.add).then_inc(s[f"acc_free{j % 2}"], 1)

        def picks(h):
            dve.wait_ge(s["sc_copied"], h // 2 + 1)
            for t in range(TB):
                for f in range(2):
                    vals, idx, src = topv[:, t, h, f, :], topi[:, t, h, f, :], sc[:, h, t, f, :]
                    ch.step(dve.max(vals[:, 0:8], src))
                    ch.wait()
                    ch.step(dve.max_index(idx[:, 0:8], vals[:, 0:8], src))
                    ch.step(dve.match_replace(sc2[:], vals[:, 0:8], src, LOWEST))
                    ch.wait()
                    ch.step(dve.max(vals[:, 8:16], sc2[:]))
                    ch.wait()
                    ch.step(dve.max_index(idx[:, 8:16], vals[:, 8:16], sc2[:]))
                c = cand[:, t, :]
                a = free(topv[:, t, h, 0, :], (1, TOPK), (0, TOPK))
                b = free(topv[:, t, h, 1, :], (0, TOPK), (1, TOPK))
                ch.step(dve.tensor_tensor(c.rearrange("p (a b) -> p a b", a=TOPK), a, b, ALU.add))
                ch.wait()
                vals, idx = cv[:, t, h, :], cpos[:, t, h, :]
                ch.step(dve.max(vals[:, 0:8], c))
                ch.wait()
                ch.step(dve.max_index(idx[:, 0:8], vals[:, 0:8], c))
                ch.step(dve.match_replace(cand2[:], vals[:, 0:8], c, LOWEST))
                ch.wait()
                ch.step(dve.max(vals[:, 8:16], cand2[:]))
                ch.wait()
                ch.step(dve.max_index(idx[:, 8:16], vals[:, 8:16], cand2[:]))

        for hc in range(NHC + 2):
            if hc < NHC:
                dve.wait_ge(s["w_hi_done"], hc + 1)
                dve.tensor_tensor(w_lo[:, hc % 2], half_source(hc), w_hi[:, hc % 2].bitcast(F32),
                                  ALU.subtract).then_inc(s["w_lo_done"], 1)
            for j in range(len(JOBS)):
                if LAST_HC[j] == hc - 1:
                    if JOBS[j][0].startswith(("na", "sg")):
                        merge(j)
                    elif JOBS[j][0].startswith("o"):
                        residual(j - JOB["o0"])
            h = hc - ATT0 - 1
            if 0 <= h < HEADS:
                logits(h)
            if 0 <= h - 1 < HEADS:
                normalise(h - 1)
            if h - 4 >= 1 and (h - 4) % 2 == 1 and h - 4 < HEADS:
                yna_split((h - 4) // 2)
            if hc == HC["sv"] + 2:
                dve.wait_ge(s["acc_free%d" % (JOB["sv"] % 2)], JOB["sv"] // 2 + 1)
                layer_norm(0, sv_sb, W5, sgn_g, sgn_b, sv_sb, s["sgln_done"], s["sgn_in"])
            if hc == HC["sg"] - 1:
                gate_spatial()
            if hc == HC["sg"]:
                ysg_split()
            if hc == HC["w0"]:
                for j in (JOB["o0"], JOB["o1"]):
                    dve.wait_ge(s[f"acc_free{j % 2}"], j // 2 + 1)
                layer_norm(1, xres, D, ln1g, ln1b, xres, s["x1_ready"], s["ln1_in"])
                split_act(6, 4)
            if HC["w0"] + 4 <= hc and (hc - HC["w0"] - 4) % 2 == 0:
                i = (hc - HC["w0"] - 4) // 2
                picks(2 * i)
                picks(2 * i + 1)
        for h in range(6, PH):
            picks(h)
        ch.wait()
        cvr = cv[:].rearrange("p t h k -> p (t h) k")
        gwr = gw[:].rearrange("p t (h k) -> p (t h) k", k=TOPK)
        dve.tensor_tensor(gwr, cvr, free(cv[:, 0, 0, :], (TOPK, TB * PH), (0, TOPK)), ALU.subtract) \
            .then_inc(s["soft_in"], 1)
        flat = cpos[:].rearrange("p t h k -> p (t h k)")
        ch.step(dve.tensor_scalar(chalf[:, 0].rearrange("p t h k -> p (t h k)"), flat, 4, None,
                                  ALU.logical_shift_right))
        ch.step(dve.tensor_scalar(chalf[:, 1].rearrange("p t h k -> p (t h k)"), flat, TOPK - 1, None,
                                  ALU.bitwise_and))
        ch.step(dve.tensor_copy(topf[:].rearrange("p t h f k -> p (t h f k)"),
                                topi[:].rearrange("p t h f k -> p (t h f k)")))
        ch.wait()
        ch.step(dve.tensor_copy(chalff[:].rearrange("p f t h k -> p (f t h k)"),
                                chalf[:].rearrange("p f t h k -> p (f t h k)")))
        ch.wait()
        for t in range(TB):
            for f, dst in enumerate((e1f, e2f)):
                e = eq[:].rearrange("p (h j) a -> p h j a", h=PH)
                rank = free(chalff[:, f, t, 0, :], (1, SLOTS), (0, TOPK))
                ch.wait()
                ch.step(dve.tensor_tensor(eq[:], rank, free(iota[:, 0:1], (0, SLOTS), (1, TOPK)), ALU.is_equal))
                keys = free(topf[:, t, 0, f, :], (2 * TOPK, PH), (0, TOPK), (1, TOPK))
                ch.wait()
                ch.step(dve.tensor_tensor(e, e, keys, ALU.mult))
                ch.wait()
                ch.step(dve.tensor_reduce(dst[:, t, :], eq[:], AX_X, ALU.add))
        dve.wait_ge(s["soft_exp"], 1)
        ch.step(dve.tensor_reduce(gsum, gwr, AX_X, ALU.add))
        ch.wait()
        ch.step(dve.reciprocal(ginv, gsum))
        ch.wait()
        dve.tensor_tensor(gwr, gwr, free(ginv, (1, TB * PH), (0, TOPK)), ALU.mult) \
            .then_inc(s["route_done"], 1)

        dve.wait_ge(s["routeT_copied"], 3)
        def onehots(i, head):
            for q in range(2):
                if not head:
                    dve.wait_ge(s["g_bank"], 2 * i + q - 1)
                for k in range(4):
                    slot = 4 * q + k
                    t = 8 * i + slot
                    dve.tensor_scalar(onehot2[:, slot, :], iota[:], e2T[:, bass.ds(t, 1)], None, ALU.is_equal)
                    ins = dve.tensor_scalar(onehot1g[:, slot, :], iota[:], e1T[:, bass.ds(t, 1)],
                                            gT[:, bass.ds(t, 1)], ALU.is_equal, ALU.mult)
                ins.then_inc(s["onehots"], 1)

        onehots(0, True)
        with dve.Fori(1, T // 8) as i:
            onehots(i, False)

        def split_uT(b, slot):
            dve.wait_ge(s["uT_hi_done"], b + 1)
            dve.tensor_tensor(uT_lo[:, slot].rearrange("p a b -> p (a b)"),
                              ps[:, 6:8, :].rearrange("p a b -> p (a b)"),
                              uT_hi[:, slot].rearrange("p a b -> p (a b)").bitcast(F32),
                              ALU.subtract).then_inc(s["uT_lo_done"], 1)

        def split_v(b, slot):
            dve.wait_ge(s["v_hi_done"], b + 1)
            dve.tensor_tensor(v_lo[:, slot, :], v_raw[:, slot, :], v_hi[:, slot, :].bitcast(F32),
                              ALU.subtract).then_inc(s["v_lo_done"], 1)

        def pair(i, head, tail):
            for slot in range(2):
                b = 2 * i + slot
                dve.wait_ge(s["act_done"], b + 1)
                dve.tensor_tensor(act_e[:, slot, :], act_e[:, slot, :], G[:, bass.ds(b * T, T)], ALU.mult) \
                    .then_inc(s["hid_m"], 1)
                dve.wait_ge(s["hid_m"], b + 1)
                if not head:
                    dve.wait_ge(s["y_done"], b - 1)
                dve.tensor_copy(hid_hi[:, slot, :], act_e[:, slot, :]).then_inc(s["hid_h"], 1)
                dve.wait_ge(s["hid_h"], b + 1)
                dve.tensor_tensor(hid_lo[:, slot, :], act_e[:, slot, :], hid_hi[:, slot, :].bitcast(F32),
                                  ALU.subtract).then_inc(s["hid_done"], 1)
                if tail and slot == 1:
                    continue
                split_uT(b + 1, 1 - slot)
                split_v(b + 1, 1 - slot)

        dve.wait_ge(s["g_bank"], T // 4)
        split_uT(0, 0)
        split_v(0, 0)
        pair(0, True, False)
        with dve.Fori(1, NB // 2 - 1) as i:
            pair(i, False, False)
        pair(NB // 2 - 1, False, True)
        dve.wait_ge(s["y_done"], NB)
        for t in range(TB):
            ch.step(dve.scalar_tensor_tensor(xres[:, t, :], xres[:, t, :], ALPHA,
                                             ps[:, 2 * t:2 * t + 2, :].rearrange("p a b -> p (a b)"),
                                             ALU.mult, ALU.add))
        layer_norm(2, xres, D, ln2g, ln2b, xres, s["out_ready"], s["ln2_in"])

    @block.tensor
    def _(pe):
        pe.wait_ge(s["ident_ready"], 3)

        def transpose_rows(ready, wait_free):
            for t, g in ((t, g) for g in range(4) for t in range(TB)):
                if t == 0:
                    wait_free(g)
                    pe.wait_ge(*ready)
                for k in range(2):
                    ins = pe.transpose(ps[:, 4 + g, k * T + t * P:k * T + (t + 1) * P],
                                       xres[:, t, (2 * g + k) * P:(2 * g + k + 1) * P], ident[:])
                if t == TB - 1:
                    ins.then_inc(s["tp_done"], 1)

        transpose_rows((s["x_in"], 16), lambda g: None)
        pe.wait_ge(s["ws_in"], 16)
        pe.wait_ge(s["act_lo_done"], 1)
        for g in range(GROUPS):
            ins = pe.transpose(ps[:, 4, g * P:(g + 1) * P], ws_raw[:, g, :], ident[:])
        ins.then_inc(s["tp_done"], 1)
        pe.wait_ge(s["sk_in"], 32)
        pe.wait_ge(s["act_lo_done"], 2)
        for f in range(2):
            ins = pe.transpose(ps[:, 5, f * P:(f + 1) * P], sk_raw[:, f, :], ident[:])
        ins.then_inc(s["tp_done"], 1)

        def scores(h):
            pe.wait_ge(s["acc_free1"], 1)
            if h == 0:
                pe.wait_ge(s["tp_copied"], 2)
            else:
                pe.wait_ge(s["logit_done"], h)
            p0 = DH * (h % 2)
            for b in range(TB):
                ins = pe.matmul(ps[:, 4, b * T:(b + 1) * T], qT[p0:p0 + DH, h // 2, b * P:(b + 1) * P],
                                kT[p0:p0 + DH, h // 2, :], start=True, stop=True)
            ins.then_inc(s["score_done"], 1)

        def transpose_probs(h):
            pe.wait_ge(s["prob_ready"], 2 * h + 2)
            if h >= 1:
                pe.wait_ge(s["probT_copied"], h)
            for kb in range(TB):
                for b in range(TB):
                    ins = pe.transpose(ps[:, 5, kb * T + b * P:kb * T + (b + 1) * P],
                                       prob[:, h % 2, b, kb * P:(kb + 1) * P], ident[:])
            ins.then_inc(s["probT_done"], 1)

        def times_v(h):
            pe.wait_ge(s["probT_copied"], h + 1)
            pe.wait_ge(s["acc_free0"], 2)
            if h >= 2 and h % 2 == 0:
                pe.wait_ge(s["yna_lo_done"], h // 2)
            p0 = DH * (h % 2)
            for kb in range(TB):
                ins = pe.matmul(ps[p0:p0 + DH, 6, 0:T], v_sb[:, kb, h * DH:(h + 1) * DH], probT[:, h % 2, kb, :],
                                start=(kb == 0), stop=(kb == TB - 1))
            ins.then_inc(s["pv_done"], 1)

        def mix():
            pe.wait_ge(s["yna_lo_done"], HEADS // 2)
            for b in range(TB):
                pe.wait_ge(s["sgln_done"], b + 1)
                for g in range(GROUPS):
                    ins = pe.matmul(ps[:, 6 + b, g * P:(g + 1) * P], wsT[:, g, :], sv_sb[:, b, g * P:(g + 1) * P],
                                    start=True, stop=True)
                ins.then_inc(s["mix_done"], 1)

        def transpose_ysg():
            pe.wait_ge(s["logit_done"], HEADS)
            pe.wait_ge(s["probT_copied"], HEADS)
            pe.wait_ge(s["ysg_done"], TB * GROUPS)
            for b2 in range(2):
                for k in range(2):
                    for t in range(TB):
                        g = 2 * b2 + k
                        ins = pe.transpose(ps[:, 4 + b2, k * T + t * P:k * T + (t + 1) * P],
                                           ysg[:, t, g * P:(g + 1) * P], ident[:])
                ins.then_inc(s["ysgT_done"], 1)

        def key_scores(i):
            j = JOB["w0"] + i
            pe.wait_ge(s[f"acc_free{j % 2}"], j // 2 + 1)
            if i == 0:
                pe.wait_ge(s["act_lo_done"], 8)
            else:
                pe.wait_ge(s["sc_copied"], i)
            for hh in range(2):
                for t in range(TB):
                    for f in range(2):
                        c = (t * 2 + f) * NK
                        ins = pe.matmul(ps[:, 4 + hh, c:c + NK], pqT[:, i % 2, 2 * hh + f, t * P:(t + 1) * P],
                                        skT[:, f, :], start=True, stop=True)
            ins.then_inc(s["key_scores"], 1)

        for hc in range(NHC + 2):
            if hc < NHC:
                j = JOB_OF_HC[hc]
                name, hcs = JOBS[j]
                first = hc == hcs[0]
                if first and j >= 2:
                    pe.wait_ge(s[f"acc_free{j % 2}"], j // 2)
                if name in ("na0", "sg0"):
                    n = {"na0": ("yna_lo_done", HEADS // 2), "sg0": ("ysgT_lo_done", 2)}[name]
                    pe.wait_ge(s[n[0]], n[1])
                if name == "o0" and first:
                    pe.wait_ge(s["mrg_lo_done"], 1)
                if name == "o0" and not first:
                    pe.wait_ge(s["mrg_lo_done"], 2)
                if name == "q" and first:
                    pe.wait_ge(s["act_lo_done"], 4)
                if name == "w0" and first:
                    pe.wait_ge(s["act_lo_done"], 8)
                pe.wait_ge(s["w_lo_done"], hc + 1)
                a_hi, a_lo = {"n": (yna_hi, yna_lo), "s": (act_hi, act_lo), "o": (mrg_hi, mrg_lo)} \
                    .get(name[0], (act_hi, act_lo))
                if name in ("sg0", "sg1"):
                    a_hi, a_lo = ysgT_hi, ysgT_lo
                k0 = KW * hcs.index(hc)
                natural = name in ("v", "sv", "su", "o0", "o1")
                a = acc(j)
                slot = hc % 2
                for m in range(TB if natural else 4):
                    for k in range(KW):
                        for part in range(3):
                            ah = (a_hi, a_lo, a_hi)[part]
                            wh = (w_hi, w_hi, w_lo)[part]
                            if natural:
                                dst = a[:, m * W5:(m + 1) * W5]
                                l = ah[:, k0 + k, m * P:(m + 1) * P]
                                r = wh[:, slot, k, :]
                                opens = first and k == 0 and part == 0
                            else:
                                dst = a[:, m * T:(m + 1) * T]
                                l = wh[:, slot, k, m * P:(m + 1) * P]
                                r = ah[:, k0 + k, :]
                                opens = first and k == 0 and part == 0 and m % 2 == 0
                            ins = pe.matmul(dst, l, r, start=opens, stop=(hc == hcs[-1] and k == KW - 1 and part == 2),
                                            skip_group_check=True)
                ins.then_inc(s["w_used"], 1)
            h = hc - ATT0
            if 0 <= h < HEADS:
                scores(h)
            if 0 <= h - 2 < HEADS:
                transpose_probs(h - 2)
            if 0 <= h - 4 < HEADS:
                times_v(h - 4)
            if hc == HC["na"]:
                mix()
            if hc == HC["sg"] - 1:
                transpose_ysg()
            if hc == HC["o1"] + 1:
                def free_bank(g):
                    pe.wait_ge(s["ysgT_lo_done"], 2)
                    pe.wait_ge(s["ysg_done"], TB * GROUPS)
                for t in range(TB):
                    pe.wait_ge(s["x1_ready"], t + 1)
                transpose_rows((s["x1_ready"], TB), free_bank)
            if hc >= HC["w0"] + 2 and (hc - HC["w0"] - 2) % 2 == 0 and (hc - HC["w0"] - 2) // 2 < 4:
                key_scores((hc - HC["w0"] - 2) // 2)

        pe.wait_ge(s["sc_copied"], 4)
        pe.wait_ge(s["route_done"], 1)
        for n, src in enumerate((e1f, e2f, gw)):
            for t in range(TB):
                ins = pe.transpose(ps[:, 4 + n, t * P:(t + 1) * P], src[:, t, :], ident[:])
        ins.then_inc(s["routeT_done"], 1)
        def gate_weights(i, head):
            for q in range(2):
                pe.wait_ge(s["onehots"], 2 * i + q + 1)
                if not head:
                    pe.wait_ge(s["g_copied"], 2 * i + q - 1)
                for k in range(4):
                    ins = pe.matmul(ps[:, q, k * NK:(k + 1) * NK], onehot2[:, 4 * q + k, :],
                                    onehot1g[:, 4 * q + k, :], start=True, stop=True)
                ins.then_inc(s["g_bank"], 1)

        gate_weights(0, True)
        with pe.Fori(1, T // 8) as i:
            gate_weights(i, False)

        def transpose_u(landed, slot):
            pe.wait_ge(s[f"u_in{slot}"], landed)
            for k in range(KD):
                ins = pe.transpose(ps[:, 6 + k // 4, (k % 4) * P:(k % 4 + 1) * P],
                                   u_raw[:, slot, k * P:(k + 1) * P], ident[:])
            ins.then_inc(s["u_read"], 1)

        def expert_inputs(slot):
            for k in range(KD):
                for part in range(3):
                    ins = pe.matmul(ps[:, 4 + slot, 0:T], (uT_hi, uT_hi, uT_lo)[part][:, slot, k, :],
                                    (act_hi, act_lo, act_hi)[part][:, k, :],
                                    start=(k == 0 and part == 0), stop=(k == KD - 1 and part == 2))
            ins.then_inc(s["a_done"], 1)

        def expert_outputs(slot, opens, closes):
            for t in range(TB):
                for part in range(3):
                    h = (hid_hi, hid_lo, hid_hi)[part][:, slot, t * P:(t + 1) * P]
                    v = (v_hi, v_hi, v_lo)[part]
                    for d in range(2):
                        ins = pe.matmul(ps[:, 2 * t + d, :], h, v[:, slot, d * 512:(d + 1) * 512],
                                        start=(opens and part == 0), stop=(closes and part == 2),
                                        skip_group_check=True)
            ins.then_inc(s["y_done"], 1)

        def pair(i, head, tail):
            for slot in range(2):
                b = 2 * i + slot
                pe.wait_ge(s["uT_lo_done"], b + 1)
                if not head:
                    pe.wait_ge(s["act_done"], b - 1)
                expert_inputs(slot)
                if not (tail and slot == 1):
                    transpose_u(16 * (i + 1) if slot == 0 else 16 * i + 32, 1 - slot)
                if not (head and slot == 0):
                    pe.wait_ge(s["hid_done"], b)
                    pe.wait_ge(s["v_lo_done"], b)
                    expert_outputs(1 - slot, head, False)

        transpose_u(16, 0)
        pe.wait_ge(s["g_copied"], T // 4)
        pair(0, True, False)
        with pe.Fori(1, NB // 2 - 1) as i:
            pair(i, False, False)
        pair(NB // 2 - 1, False, True)
        pe.wait_ge(s["hid_done"], NB)
        pe.wait_ge(s["v_lo_done"], NB)
        expert_outputs(1, False, True)

    blocks.__exit__(None, None, None)


_INS = ["x", "w_in", "na_rpb", "sg_norm_g", "sg_norm_b", "sg_spatial_w", "sg_spatial_b", "w_branch_na",
        "w_branch_sg", "w_out", "ln1_g", "ln1_b", "peer_wq", "peer_subkeys1", "peer_subkeys2", "peer_u",
        "peer_v", "ln2_g", "ln2_b"]
_OUTS = [((1, T, D), "float32")]


def kernel(**inputs):
    import numpy as _np
    import concourse.bacc as _bacc
    from concourse import mybir as _mybir
    from concourse.bass_utils import run_bass_kernel_spmd as _run

    nc = _bacc.Bacc("TRN2", target_bir_lowering=False, num_devices=1)
    arrays, args = {}, []
    for name in _INS:
        a = inputs[name]
        if name == "na_rpb":
            a = _np.asarray(a)[:, :, ::-1, ::-1]
        a = _np.ascontiguousarray(a)
        arrays[f"in_{name}_dram"] = a
        args.append(nc.dram_tensor(f"in_{name}_dram", a.shape, _mybir.dt.from_np(a.dtype), kind="ExternalInput").ap())
    for i, (shape, dtype) in enumerate(_OUTS):
        dt = _mybir.dt.from_np(_np.dtype(dtype))
        args.append(nc.dram_tensor(f"out_{i}_dram", shape, dt, kind="ExternalOutput").ap())
    hybrid_block(nc, *args)
    r = _run(nc, [arrays], core_ids=[0])
    got = tuple(r.results[0][f"out_{i}_dram"] for i in range(len(_OUTS)))
    return got[0]
```

```python
import math

import concourse.bass as bass
from concourse import mybir

F32 = mybir.dt.float32
F32R = mybir.dt.float32r
U32 = mybir.dt.uint32
ALU = mybir.AluOpType
ACT = mybir.ActivationFunctionType
AX_X = mybir.AxisListType.X

P = 128
D = 1024
T = 256
TB = T // P
KD = D // P
HEADS, DH = 8, 64
GRID_W, ROWS = 64, T // 64
WIN_H, WIN_W = 8, 16
RPB_W = 2 * WIN_W - 1
RPB_H = 2 * WIN_H - 1
W5 = 512
KW = W5 // P
GROUPS = 4
PH = 8
NK = 128
TOPK = 16
SLOTS = PH * TOPK
NEXP = NK * NK
ALPHA = 2.0 ** 0.25
EPS = 1e-5
LOWEST = -3.0e38
MASKED = -1.0e30
NB = NK
NPRE = 48
NDUR = 32
NEARLY = NPRE + NDUR
PARTS = 4
PT = T // PARTS
PB = NDUR // PARTS

CHUNKS = ["q", "k", "v", "ga0", "ga1", "gb0", "gb1", "sv", "su", "na", "sg", "o0", "o1", "w0", "w1", "w2", "w3"]
COL0 = {"q": 0, "k": W5, "v": 2 * W5, "su": 3 * W5, "sv": 4 * W5,
        "ga0": 5 * W5, "ga1": 6 * W5, "gb0": 7 * W5, "gb1": 8 * W5}
NHC = 2 * len(CHUNKS)
JOBS = []
for _c, _n in enumerate(CHUNKS):
    if _n in ("na", "sg"):
        JOBS += [(_n + "0", [2 * _c]), (_n + "1", [2 * _c + 1])]
    else:
        JOBS.append((_n, [2 * _c, 2 * _c + 1]))
JOB = {n: j for j, (n, _) in enumerate(JOBS)}
JOB_OF_HC = {h: j for j, (_, hs) in enumerate(JOBS) for h in hs}
LAST_HC = {j: hs[-1] for j, (_, hs) in enumerate(JOBS)}
HC = {n: 2 * c for c, n in enumerate(CHUNKS)}
ATT0 = HC["ga0"]


PICKS_AT = {HC["w2"]: [0, 1], HC["w2"] + 1: [2, 3], HC["w3"]: [4, 5, 6], HC["w3"] + 1: [7, 8, 9]}
PICKED = 10


def free(ap, *dims, start=0):
    return bass.AP(ap.tensor, ap.offset + start, [list(ap.ap[0]), *[list(d) for d in dims]])


def hybrid_block(nc, x, w_in, na_rpb, sg_norm_g, sg_norm_b, sg_spatial_w, sg_spatial_b, w_branch_na,
                 w_branch_sg, w_out, ln1_g, ln1_b, peer_wq, peer_subkeys1, peer_subkeys2, peer_u,
                 peer_v, ln2_g, ln2_b, out):
    K1 = 1024
    base = 16512

    def sb(name, shape, at, dt=F32):
        return nc.alloc_sbuf_tensor_at(name, shape, dt, offset=base + int(at))

    ident = sb("ident", [P, P], 0)
    iota = sb("iota", [P, P], 512)
    act_hi = sb("act_hi", [P, KD, T], 1 * K1, F32R)
    act_lo = sb("act_lo", [P, KD, T], 9 * K1, F32R)
    xres = sb("xres", [P, TB, D], 17 * K1)
    w_raw = sb("w_raw", [P, 2, 2 * KW * W5], 25 * K1)
    w_hi = sb("w_hi", [P, 2, KW, W5], 57 * K1, F32R)
    w_lo = sb("w_lo", [P, 2, KW, W5], 73 * K1, F32R)
    qT = sb("qT", [P, KW, T], 89 * K1)
    kT = sb("kT", [P, KW, T], 93 * K1)
    v_sb = sb("v_sb", [P, TB, W5], 97 * K1)
    sv_sb = sb("sv_sb", [P, TB, W5], 101 * K1)
    su_sb = sb("su_sb", [P, TB, W5], 105 * K1)
    ysg = sb("ysg", [P, TB, W5], 109 * K1)
    ws_raw = sb("ws_raw", [P, GROUPS, P], 113 * K1)
    wsT = sb("wsT", [P, GROUPS, P], 115 * K1)
    sgn_g = sb("sgn_g", [P, W5], 117 * K1)
    sgn_b = sb("sgn_b", [P, W5], 119 * K1)
    bias = sb("bias", [P, HEADS, TB, T], 121 * K1)
    mrg_hi = sb("mrg_hi", [P, KD, T], 121 * K1, F32R)
    mrg_lo = sb("mrg_lo", [P, KD, T], 129 * K1, F32R)
    prob = sb("prob", [P, 2, TB, T], 137 * K1)
    probT = sb("probT", [P, 2, TB, T], 141 * K1)
    yna_hi = sb("yna_hi", [P, KW, T], 145 * K1, F32R)
    yna_lo = sb("yna_lo", [P, KW, T], 149 * K1, F32R)
    ysgT_hi = sb("ysgT_hi", [P, KW, T], 153 * K1, F32R)
    ysgT_lo = sb("ysgT_lo", [P, KW, T], 157 * K1, F32R)
    gates = sb("gates", [P, 2 * KD, T], 161 * K1)
    ln1g = sb("ln1g", [P, D], 177 * K1)
    ln1b = sb("ln1b", [P, D], 181 * K1)
    sk_raw = sb("sk_raw", [P, 2, P], 185 * K1)
    skT = sb("skT", [P, 2, P], 186 * K1)
    pqT = sb("pqT", [P, 2, KW, T], 161 * K1)
    sc = sb("sc", [P, PH, TB, 2, NK], 89 * K1)
    eq = sb("eq", [P, SLOTS, TOPK], 25 * K1)
    e1f = sb("e1f", [P, TB, SLOTS], 187 * K1)
    e2f = sb("e2f", [P, TB, SLOTS], 188 * K1)
    gw = sb("gw", [P, TB, SLOTS], 189 * K1)
    topv = sb("topv", [P, TB, PH, 2, TOPK], 190 * K1)
    topi = sb("topi", [P, TB, PH, 2, TOPK], 192 * K1, U32)
    topf = sb("topf", [P, TB, PH, 2, TOPK], 194 * K1)
    cand = sb("cand", [P, 2, TOPK * TOPK], 196 * K1)
    cand2 = sb("cand2", [P, TOPK * TOPK], 198 * K1)
    sc2 = sb("sc2", [P, NK], 199 * K1)
    cv = sb("cv", [P, TB, PH, TOPK], 200 * K1)
    cpos = sb("cpos", [P, TB, PH, TOPK], 201 * K1, U32)
    chalf = sb("chalf", [P, 2, TB, PH, TOPK], 202 * K1, U32)
    chalff = sb("chalff", [P, 2, TB, PH, TOPK], 204 * K1)
    G = sb("G", [P, NK * T], 25 * K1)
    onehot2 = sb("onehot2", [P, 8, NK], 193 * K1)
    onehot1g = sb("onehot1g", [P, 8, NK], 197 * K1)
    e1T = sb("e1T", [P, T], 204 * K1)
    e2T = sb("e2T", [P, T], 205 * K1)
    gT = sb("gT", [P, T], 206 * K1)
    early = sb("early", [P, PB, T], 185 * K1)
    u_raw = sb("u_raw", [P, 2, D], 153 * K1)
    v_raw = sb("v_raw", [P, 2, D], 161 * K1)
    uT_hi = sb("uT_hi", [P, 2, KD, P], 169 * K1, F32R)
    uT_lo = sb("uT_lo", [P, 2, KD, P], 177 * K1, F32R)
    uT3_hi = sb("uT3_hi", [P, KD, P], 161 * K1, F32R)
    uT3_lo = sb("uT3_lo", [P, KD, P], 165 * K1, F32R)
    v_hi = sb("v_hi", [P, 2, D], 185 * K1, F32R)
    v_lo = sb("v_lo", [P, 2, D], 193 * K1, F32R)
    act_e = sb("act_e", [P, 2, T], 201 * K1)
    hid_hi = sb("hid_hi", [P, 2, T], 203 * K1, F32R)
    hid_lo = sb("hid_lo", [P, 2, T], 205 * K1, F32R)
    ln2g = sb("ln2g", [P, D], 25 * K1)
    ln2b = sb("ln2b", [P, D], 29 * K1)
    small = sb("small", [P, 84], 207 * K1)
    stats = small[:, 0:24]
    mv = small[:, 24:28]
    rstd = small[:, 28:30]
    rmax = small[:, 32:36]
    rsum = small[:, 36:40]
    rinv = small[:, 40:44]
    eps = small[:, 44:45]
    bsT = small[:, 48:52]
    gsum = small[:, 52:68]
    ginv = small[:, 68:84]

    ps = nc.psum_tensor("ps", [P, 8, 512], F32).__enter__()

    def acc(j):
        return ps[:, 2 * (j % 2):2 * (j % 2) + 2, :].rearrange("p a b -> p (a b)")

    names = ["x_in", "rpb_in", "ws_in", "bs_in", "sgn_in", "ln1_in", "sk_in", "ln2_in",
             "w_in0", "w_in1", "w_hi_done", "w_lo_done", "w_used", "acc_free0", "acc_free1",
             "pool_done", "mask_done", "ident_ready", "tp_done", "tp_hi", "tp_lo", "tp_copied", "score_done", "logit_done",
             "max_done", "exp_done", "prob_ready", "probT_done", "probT_copied", "pv_done", "yna_hi_done",
             "yna_lo_done", "gelu_done", "mix_done", "sgln_done", "ysg_done", "ysgT_done", "ysgT_hi_done",
             "ysgT_lo_done", "merged_sum", "mrg_hi_done", "mrg_lo_done", "ln_var", "ln_std", "x1_ready",
             "act_hi_done", "act_lo_done", "key_scores", "sc_copied", "soft_in", "soft_exp", "route_done",
             "routeT_done", "routeT_copied", "onehots", "g_bank", "g_copied", "g_scaled", "settled_mult", "settled_copy",
             "u_in0", "u_in1", "v_in0", "v_in1", "u_read", "uT_hi_done", "uT_lo_done", "v_hi_done",
             "v_lo_done", "a_done", "act_done", "hid_done", "hid_m", "hid_h", "y_done", "z_done", "out_ready",
             "stored", "dve"]
    s = {n: nc.semaphore(n).__enter__() for n in names}

    class Chain:

        def __init__(self, eng, sem):
            self.eng, self.sem, self.n = eng, sem, 0

        def step(self, ins):
            ins.then_inc(self.sem, 1)
            self.n += 1
            return self.n

        def wait(self, n=None):
            self.eng.wait_ge(self.sem, self.n if n is None else n)

    u_dram = peer_u[0]
    v_dram = peer_v[0]

    def chunk_source(n):
        if n in COL0:
            return w_in[0, :, COL0[n]:COL0[n] + W5].rearrange("(k p) n -> p k n", p=P)
        if n in ("na", "sg"):
            w = w_branch_na if n == "na" else w_branch_sg
            return w[0].rearrange("(k p) n -> p k n", p=P)
        w = w_out if n[0] == "o" else peer_wq
        c = int(n[1]) * W5
        return w[0, :, c:c + W5].rearrange("(k p) n -> p k n", p=P)

    def half_source(hc):
        c = hc // 2
        raw = w_raw[:, c % 2, :]
        if CHUNKS[c] in ("na", "sg"):
            return raw.rearrange("p (k n) -> p k n", k=KW)[:, :, (hc % 2) * W5:(hc % 2 + 1) * W5]
        return raw.rearrange("p (k n) -> p k n", k=KD)[:, (hc % 2) * KW:(hc % 2 + 1) * KW, :]

    blocks = nc.Block()
    block = blocks.__enter__()

    @block.sync
    def _(sp):
        sp.dma_start(xres[:], x[0].rearrange("(b p) d -> p b d", p=P)).then_inc(s["x_in"], 16)
        for c, n in enumerate(CHUNKS):
            if c >= 2:
                sp.wait_ge(s["w_lo_done"], 2 * (c - 1))
            k = KW if n in ("na", "sg") else KD
            sp.dma_start(w_raw[:, c % 2, :].rearrange("p (k n) -> p k n", k=k), chunk_source(n)) \
                .then_inc(s[f"w_in{c % 2}"], 16)
            if c == 0:
                sp.dma_start(ws_raw[:], sg_spatial_w[0].rearrange("g p q -> p g q")).then_inc(s["ws_in"], 16)
                sp.dma_start(sk_raw[:, 0, :], peer_subkeys1[0]).then_inc(s["sk_in"], 16)
                sp.dma_start(sk_raw[:, 1, :], peer_subkeys2[0]).then_inc(s["sk_in"], 16)
            if c == 1:
                for h in range(HEADS):
                    for r in range(ROWS):
                        at = (h * RPB_H + WIN_H - ROWS + r) * RPB_W + WIN_W - GRID_W
                        src = bass.AP(na_rpb.tensor, na_rpb.offset + at,
                                      [[1, GRID_W], [RPB_W, ROWS], [1, GRID_W]])
                        b, p0 = r // 2, GRID_W * (r % 2)
                        dst = bias[p0:p0 + GRID_W, h, b, :].rearrange("p (r c) -> p r c", r=ROWS)
                        sp.dma_start(dst, src).then_inc(s["rpb_in"], 16)
                sp.dma_start(bsT, sg_spatial_b[0].rearrange("g p -> p g"),
                             allow_slow_non_contiguous=True).then_inc(s["bs_in"], 16)
                sp.dma_start(sgn_g[:], sg_norm_g[0:1, :].broadcast_to([P, W5])).then_inc(s["sgn_in"], 16)
                sp.dma_start(sgn_b[:], sg_norm_b[0:1, :].broadcast_to([P, W5])).then_inc(s["sgn_in"], 16)
                sp.dma_start(ln1g[:], ln1_g[0:1, :].broadcast_to([P, D])).then_inc(s["ln1_in"], 16)
                sp.dma_start(ln1b[:], ln1_b[0:1, :].broadcast_to([P, D])).then_inc(s["ln1_in"], 16)

        def load_u(b, slot):
            sp.dma_start(u_raw[:, slot, :], u_dram[bass.ds(b * P, P), :]).then_inc(s[f"u_in{slot}"], 16)

        def load_v(b, slot):
            sp.dma_start(v_raw[:, slot, :], v_dram[bass.ds(b * P, P), :]).then_inc(s[f"v_in{slot}"], 16)

        sp.wait_ge(s["mrg_lo_done"], 2)
        for slot in range(2):
            load_u(NB - NPRE + slot, slot)
        with sp.Fori(1, NPRE // 2) as i:
            for slot in range(2):
                sp.wait_ge(s["u_read"], 2 * i + slot - 1)
                load_u(2 * i + (NB - NPRE + slot), slot)
        sp.wait_ge(s["a_done"], NPRE)
        for slot in range(2):
            load_v(NB - NEARLY + slot, slot)
        for part in range(PARTS):
            with sp.Fori(0, PB // 2) as i:
                for slot in range(2):
                    sp.wait_ge(s["u_read"], 2 * i + (NPRE + PB * part + slot - 1))
                    load_u(2 * i + (NB - NPRE - PB * (part + 1) + slot), slot)
        for slot in range(2):
            sp.wait_ge(s["u_read"], NEARLY + slot - 1)
            load_u(slot, slot)
        with sp.Fori(1, NEARLY // 2) as i:
            for slot in range(2):
                sp.wait_ge(s["v_lo_done"], 4 * i + (2 * slot - 2))
                load_v(2 * i + (NB - NEARLY + slot), slot)
        for slot in range(2):
            sp.wait_ge(s["v_lo_done"], 2 * (NEARLY + slot - 1))
            load_v(slot, slot)
        with sp.Fori(1, (NB - NEARLY) // 2) as i:
            for slot in range(2):
                sp.wait_ge(s["u_read"], 2 * i + (NEARLY + slot - 1))
                load_u(2 * i + slot, slot)
                sp.wait_ge(s["v_lo_done"], 4 * i + 2 * (NEARLY + slot - 1))
                load_v(2 * i + slot, slot)
        sp.wait_ge(s["hid_h"], NB)
        sp.dma_start(ln2g[:], ln2_g[0:1, :].broadcast_to([P, D])).then_inc(s["ln2_in"], 16)
        sp.dma_start(ln2b[:], ln2_b[0:1, :].broadcast_to([P, D])).then_inc(s["ln2_in"], 16)
        for b in range(TB):
            sp.wait_ge(s["out_ready"], b + 1)
            sp.dma_start(out[0, b * P:(b + 1) * P, :], xres[:, b, :]).then_inc(s["stored"], 16)
        sp.wait_ge(s["stored"], 16 * TB)

    @block.gpsimd
    def _(pool):
        pool.memset(ident[:], 0.0).then_inc(s["pool_done"], 1)
        pool.wait_ge(s["pool_done"], 1)
        pool.affine_select(out=ident[:], in_=ident[:], compare_op=ALU.not_equal, fill=1.0, base=0,
                           pattern=[[-1, P]], channel_multiplier=1).then_inc(s["ident_ready"], 1)
        pool.wait_ge(s["ident_ready"], 1)
        pool.iota(iota[:], [[1, P]], base=0, channel_multiplier=0,
                  allow_small_or_imprecise_dtypes=True).then_inc(s["ident_ready"], 1)
        pool.wait_ge(s["ident_ready"], 2)
        pool.memset(eps, EPS).then_inc(s["ident_ready"], 1)
        pool.wait_ge(s["ident_ready"], 3)
        pool.wait_ge(s["rpb_in"], 16 * ROWS * HEADS)
        rows = HEADS * TB * ROWS
        for n, p0 in enumerate((0, GRID_W)):
            if n:
                pool.wait_ge(s["mask_done"], 1)
            both = bias[p0:p0 + GRID_W].rearrange("p h b (r c) -> p (h b r) c", c=GRID_W)
            low = both[:, :, WIN_W:GRID_W]
            pool.affine_select(out=low, in_=low, compare_op=ALU.is_ge, fill=MASKED,
                               base=GRID_W - 1 - WIN_W + WIN_W // 2,
                               pattern=[[0, rows], [-1, GRID_W - WIN_W]],
                               channel_multiplier=-1).then_inc(s["mask_done"], 1)
        for n, p0 in enumerate((0, GRID_W)):
            both = bias[p0:p0 + GRID_W].rearrange("p h b (r c) -> p (h b r) c", c=GRID_W)
            high = both[:, :, 0:GRID_W - WIN_W]
            pool.wait_ge(s["mask_done"], n + 2)
            pool.affine_select(out=high, in_=high, compare_op=ALU.is_ge, fill=MASKED,
                               base=WIN_W // 2 - GRID_W,
                               pattern=[[0, rows], [1, GRID_W - WIN_W]],
                               channel_multiplier=1).then_inc(s["mask_done"], 1)

    @block.scalar
    def _(act):
        def split_act(n, first_tp):
            for g in range(4):
                act.wait_ge(s["tp_done"], first_tp + g + 1)
                act.activation(act_hi[:, 2 * g:2 * g + 2, :].rearrange("p a b -> p (a b)"), ps[:, 4 + g, :],
                               ACT.Copy).then_inc(s["act_hi_done"], 1)

        split_act(0, 0)
        act.wait_ge(s["tp_done"], 5)
        act.activation(wsT[:].rearrange("p a b -> p (a b)"), ps[:, 4, :], ACT.Copy).then_inc(s["tp_copied"], 1)
        act.wait_ge(s["tp_done"], 6)
        act.activation(skT[:].rearrange("p a b -> p (a b)"), ps[:, 5, 0:2 * P], ACT.Copy) \
            .then_inc(s["tp_copied"], 1)

        def free_acc(ins, j):
            ins.then_inc(s[f"acc_free{j % 2}"], 1)

        def evacuate(j):
            name = JOBS[j][0]
            a = acc(j)
            act.wait_ge(s["w_used"], LAST_HC[j] + 1)
            if name in ("q", "k", "v"):
                dst = {"q": qT, "k": kT, "v": v_sb}[name]
                free_acc(act.activation(dst[:].rearrange("p a b -> p (a b)"), a, ACT.Copy), j)
            elif name[0] == "g":
                i = j - JOB["ga0"]
                dst = gates[:, 4 * i:4 * i + 4, :].rearrange("p a b -> p (a b)")
                free_acc(act.activation(dst, a, ACT.Tanh, scale=0.5), j)
            elif name in ("sv", "su"):
                dst = sv_sb if name == "sv" else su_sb
                free_acc(act.activation(dst[:].rearrange("p a b -> p (a b)"), a, ACT.Gelu_apprx_tanh), j)
            elif name in ("w0", "w1", "w2", "w3"):
                i = int(name[1])
                if i >= 2:
                    act.wait_ge(s["key_scores"], i - 1)
                free_acc(act.activation(pqT[:, i % 2].rearrange("p a b -> p (a b)"), a, ACT.Copy), j)

        def attention_exp(h):
            act.wait_ge(s["max_done"], h + 1)
            for b in range(TB):
                act.activation(prob[:, h % 2, b, :], prob[:, h % 2, b, :], ACT.Exp,
                               bias=rmax[:, 2 * (h % 2) + b:2 * (h % 2) + b + 1],
                               accum_out=rsum[:, 2 * (h % 2) + b:2 * (h % 2) + b + 1]).then_inc(s["exp_done"], 1)

        def copy_probT(h):
            act.wait_ge(s["probT_done"], h + 1)
            if h >= 2:
                act.wait_ge(s["pv_done"], h - 1)
            act.activation(probT[:, h % 2].rearrange("p a b -> p (a b)"), ps[:, 5, :], ACT.Copy) \
                .then_inc(s["probT_copied"], 1)

        def yna_split(pair):
            act.wait_ge(s["pv_done"], 2 * pair + 2)
            act.activation(yna_hi[:, pair, :], ps[:, 6, 0:T], ACT.Copy).then_inc(s["yna_hi_done"], 1)

        def ysg_split():
            for b in range(2):
                act.wait_ge(s["ysgT_done"], b + 1)
                act.activation(ysgT_hi[:, 2 * b:2 * b + 2, :].rearrange("p a b -> p (a b)"), ps[:, 4 + b, :],
                               ACT.Copy).then_inc(s["ysgT_hi_done"], 1)

        def sqrt_var(n, cols):
            act.wait_ge(s["ln_var"], TB * (n + 1))
            act.activation(rstd[:, 0:cols], mv.rearrange("p (b s) -> p b s", s=2)[:, 0:cols, 1], ACT.Sqrt,
                           bias=eps).then_inc(s["ln_std"], 1)

        def copy_scores(i):
            act.wait_ge(s["key_scores"], i + 1)
            act.activation(sc[:, 2 * i:2 * i + 2].rearrange("p a b c d -> p (a b c d)"),
                           ps[:, 4:6, :].rearrange("p a b -> p (a b)"), ACT.Copy).then_inc(s["sc_copied"], 1)

        for hc in range(NHC + 2):
            if hc < NHC:
                c = hc // 2
                act.wait_ge(s[f"w_in{c % 2}"], 16 * (c // 2 + 1))
                if hc >= 2:
                    act.wait_ge(s["w_used"], hc - 1)
                act.activation(w_hi[:, hc % 2], half_source(hc), ACT.Copy).then_inc(s["w_hi_done"], 1)
            for j in range(len(JOBS)):
                if LAST_HC[j] == hc - 1 and not JOBS[j][0].startswith(("na", "sg", "o")):
                    evacuate(j)
            h = hc - ATT0 - 1
            if 0 <= h < HEADS:
                attention_exp(h)
            if 0 <= h - 2 < HEADS:
                copy_probT(h - 2)
            if h - 4 >= 1 and (h - 4) % 2 == 1 and h - 4 < HEADS:
                yna_split((h - 4) // 2)
            if hc == HC["sv"] + 2:
                sqrt_var(0, TB)
            if hc == HC["sg"]:
                ysg_split()
            if hc in (HC["sg"] + 1, HC["sg"] + 2):
                i = hc - HC["sg"] - 1
                act.wait_ge(s["merged_sum"], i + 1)
                act.activation(mrg_hi[:, 4 * i:4 * i + 4, :].rearrange("p a b -> p (a b)"),
                               gates[:, 4 * i:4 * i + 4, :].rearrange("p a b -> p (a b)"), ACT.Copy,
                               scale=0.5).then_inc(s["mrg_hi_done"], 1)
            if hc == HC["w0"]:
                sqrt_var(1, TB)
                split_act(1, 6)
            if HC["w0"] + 3 <= hc and (hc - HC["w0"] - 3) % 2 == 0 and (hc - HC["w0"] - 3) // 2 < 4:
                copy_scores((hc - HC["w0"] - 3) // 2)
        def round_uT(n, banks, dst):
            act.wait_ge(s["u_read"], n + 1)
            act.activation(dst.rearrange("p a b -> p (a b)"), ps[:, banks:banks + 2, :].rearrange("p a b -> p (a b)"),
                           ACT.Copy).then_inc(s["uT_hi_done"], 1)

        def pre_slot(k):
            return uT3_hi[:] if k % 3 == 2 else uT_hi[:, k % 3]

        def pre_six(i, last):
            for k in range(6):
                if not (last and k >= 4):
                    round_uT(6 * i + k + 2, 6 - 4 * (k % 2), pre_slot(k + 2))
                act.wait_ge(s["a_done"], 6 * i + k + 1)
                act.activation(G[:, bass.ds((6 * i + (NB - NPRE + k)) * T, T)], ps[:, k % 2, 0:T],
                               ACT.Gelu_apprx_tanh).then_inc(s["act_done"], 1)

        round_uT(0, 6, pre_slot(0))
        round_uT(1, 2, pre_slot(1))
        with act.Fori(0, NPRE // 6 - 1) as i:
            pre_six(i, False)
        pre_six(NPRE // 6 - 1, True)

        act.wait_ge(s["soft_in"], 1)
        act.activation(gw[:].rearrange("p a b -> p (a b)"), gw[:].rearrange("p a b -> p (a b)"), ACT.Exp) \
            .then_inc(s["soft_exp"], 1)
        act.wait_ge(s["routeT_done"], 1)
        for n, dst in enumerate((e1T, e2T, gT)):
            act.activation(dst[:], ps[:, 4 + n, 0:T], ACT.Copy).then_inc(s["routeT_copied"], 1)
        G3 = G[:].rearrange("p (e t) -> p e t", t=T)

        def during(part, i, slot):
            h = PB * part + 2 * i + slot
            n = NPRE + h
            todo = NB - NPRE - PB * part
            round_uT(n + 1, 6, uT_hi[:, 1 - slot])
            act.wait_ge(s["a_done"], n + 1)
            act.activation(early[:].rearrange("p a b -> p (a b)")[:, bass.ds((2 * i + slot) * T, T)],
                           ps[:, 4 + slot, 0:T], ACT.Gelu_apprx_tanh).then_inc(s["act_done"], 1)
            for q in range(2):
                act.wait_ge(s["g_bank"], 2 * h + q + 1)
                act.activation(G3[:, 0:todo, bass.ds(8 * h + 4 * q, 4)],
                               ps[:, 2 * slot + q, :].rearrange("p (t e) -> p e t", t=4)[:, 0:todo, :], ACT.Copy) \
                    .then_inc(s["g_copied"], 1)

        round_uT(NPRE, 6, uT_hi[:, 0])
        for part in range(PARTS):
            if part:
                act.wait_ge(s["settled_mult"], part)
            with act.Fori(0, PB // 2) as i:
                for slot in range(2):
                    during(part, i, slot)
            top = NB - NPRE - PB * part
            if part < PARTS - 1:
                act.wait_ge(s["act_done"], NPRE + PB * (part + 1))
                act.activation(G3[:, top - PB:top, PT * (part + 1):T], early[:, :, PT * (part + 1):T], ACT.Copy) \
                    .then_inc(s["settled_copy"], 1)
                act.wait_ge(s["settled_copy"], part + 1)

        def round_v(slot, landed):
            act.wait_ge(s[f"v_in{slot}"], landed)
            for d in range(2):
                act.activation(v_hi[:, slot, d * 512:(d + 1) * 512], v_raw[:, slot, d * 512:(d + 1) * 512],
                               ACT.Copy).then_inc(s["v_hi_done"], 1)

        act.wait_ge(s["settled_mult"], PARTS)
        for slot in range(2):
            round_v(slot, 16)
        with act.Fori(1, NEARLY // 2) as i:
            for slot in range(2):
                act.wait_ge(s["y_done"], 2 * i + slot - 1)
                round_v(slot, 16 * i + 16)
        act.wait_ge(s["y_done"], NEARLY - 1)
        round_v(0, 16 * (NEARLY // 2) + 16)

        def pair(i, head, tail):
            for slot in range(2):
                n = 2 * i + slot
                act.wait_ge(s["a_done"], n + 1)
                if not head:
                    act.wait_ge(s["hid_done"], n - 1)
                act.activation(act_e[:, slot, :], ps[:, 4 + slot, 0:T], ACT.Gelu_apprx_tanh) \
                    .then_inc(s["act_done"], 1)
                if tail and slot == 1:
                    continue
                round_uT(n + 1, 6, uT_hi[:, 1 - slot])
                act.wait_ge(s["y_done"], n)
                round_v(1 - slot, 16 * i + 16 if slot == 0 else 16 * i + 32)

        pair(NEARLY // 2, True, False)
        with act.Fori(NEARLY // 2 + 1, NB // 2 - 1) as i:
            pair(i, False, False)
        pair(NB // 2 - 1, False, True)
        sqrt_var(2, TB)

    @block.vector
    def _(dve):
        ch = Chain(dve, s["dve"])

        def split_act(first_tp, first_hi):
            for g in range(4):
                dve.wait_ge(s["act_hi_done"], first_hi + g + 1)
                dst = act_lo[:, 2 * g:2 * g + 2, :].rearrange("p a b -> p (a b)")
                hi = act_hi[:, 2 * g:2 * g + 2, :].rearrange("p a b -> p (a b)").bitcast(F32)
                dve.tensor_tensor(dst, ps[:, 4 + g, :], hi, ALU.subtract).then_inc(s["act_lo_done"], 1)

        def layer_norm(n, src, width, g, b, dst, done, gb_in, blocks=TB):
            parts = width // 512
            ch.wait()
            for t in range(blocks):
                for q in range(parts):
                    ch.step(dve.bn_stats(stats[:, 12 * t + 6 * q:12 * t + 6 * q + 6],
                                         src[:, t, 512 * q:512 * q + 512]))
            for t in range(blocks):
                ch.wait()
                dve.bn_aggr(mv[:, 2 * t:2 * t + 2], stats[:, 12 * t:12 * t + 6 * parts]) \
                    .then_inc(s["ln_var"], 1)
            dve.wait_ge(s["ln_std"], n + 1)
            ch.step(dve.reciprocal(rstd[:, 0:2], rstd[:, 0:2]))
            ch.wait()
            dve.wait_ge(gb_in, 32)
            for t in range(blocks):
                ch.step(dve.tensor_scalar(dst[:, t, :], src[:, t, :], mv[:, 2 * t:2 * t + 1],
                                          rstd[:, t:t + 1], ALU.subtract, ALU.mult))
                ch.wait()
                ch.step(dve.tensor_tensor(dst[:, t, :], dst[:, t, :], g[:], ALU.mult))
                ch.wait()
                dve.tensor_tensor(dst[:, t, :], dst[:, t, :], b[:], ALU.add).then_inc(done, 1)

        split_act(0, 0)

        def logits(h):
            dve.wait_ge(s["score_done"], h + 1)
            dve.wait_ge(s["mask_done"], 4)
            if h >= 2:
                dve.wait_ge(s["probT_done"], h - 1)
            dve.scalar_tensor_tensor(prob[:, h % 2], ps[:, 4, :].rearrange("p (b k) -> p b k", b=TB), DH ** -0.5,
                                     free(bias[:, h, 0, :], (T, TB), (-1, T), start=T - 1),
                                     ALU.mult, ALU.add).then_inc(s["logit_done"], 1)
            dve.wait_ge(s["logit_done"], h + 1)
            m = rmax[:, 2 * (h % 2):2 * (h % 2) + 2]
            ch.step(dve.tensor_reduce(m, prob[:, h % 2], AX_X, ALU.max))
            ch.wait()
            dve.tensor_scalar(m, m, -1.0, None, ALU.mult).then_inc(s["max_done"], 1)

        def normalise(h):
            dve.wait_ge(s["exp_done"], 2 * h + 2)
            r = rinv[:, 2 * (h % 2):2 * (h % 2) + 2]
            ch.step(dve.reciprocal(r, rsum[:, 2 * (h % 2):2 * (h % 2) + 2]))
            ch.wait()
            for b in range(TB):
                dve.tensor_scalar(prob[:, h % 2, b, :], prob[:, h % 2, b, :], r[:, b:b + 1], None,
                                  ALU.mult).then_inc(s["prob_ready"], 1)

        def yna_split(pair):
            dve.wait_ge(s["yna_hi_done"], pair + 1)
            dve.tensor_tensor(yna_lo[:, pair, :], ps[:, 6, 0:T], yna_hi[:, pair, :].bitcast(F32),
                              ALU.subtract).then_inc(s["yna_lo_done"], 1)

        def gate_spatial():
            dve.wait_ge(s["bs_in"], 16)
            dve.wait_ge(s["acc_free%d" % (JOB["su"] % 2)], JOB["su"] // 2 + 1)
            for b in range(TB):
                dve.wait_ge(s["mix_done"], b + 1)
                for g in range(GROUPS):
                    dve.scalar_tensor_tensor(ysg[:, b, g * P:(g + 1) * P], ps[:, 6 + b, g * P:(g + 1) * P],
                                             bsT[:, g:g + 1], su_sb[:, b, g * P:(g + 1) * P],
                                             ALU.add, ALU.mult).then_inc(s["ysg_done"], 1)

        def ysg_split():
            for b in range(2):
                dve.wait_ge(s["ysgT_hi_done"], b + 1)
                hi = ysgT_hi[:, 2 * b:2 * b + 2, :].rearrange("p a b -> p (a b)").bitcast(F32)
                dve.tensor_tensor(ysgT_lo[:, 2 * b:2 * b + 2, :].rearrange("p a b -> p (a b)"),
                                  ps[:, 4 + b, :], hi, ALU.subtract).then_inc(s["ysgT_lo_done"], 1)

        def merge(j):
            name = JOBS[j][0]
            dve.wait_ge(s["w_used"], LAST_HC[j] + 1)
            i = int(name[-1])
            ga = gates[:, 4 * i:4 * i + 4, :].rearrange("p a b -> p (a b)")
            gb = gates[:, 8 + 4 * i:12 + 4 * i, :].rearrange("p a b -> p (a b)")
            if name[:2] == "na":
                dve.wait_ge(s[f"acc_free{(JOB['gb1']) % 2}"], JOB["gb1"] // 2 + 1)
                dve.wait_ge(s[f"acc_free{(JOB['gb0']) % 2}"], JOB["gb0"] // 2 + 1)
                ins = dve.scalar_tensor_tensor(ga, ga, 1.0, acc(j), ALU.add, ALU.mult)
                ins.then_inc(s[f"acc_free{j % 2}"], 1)
            else:
                dve.scalar_tensor_tensor(gb, gb, 1.0, acc(j), ALU.add, ALU.mult) \
                    .then_inc(s[f"acc_free{j % 2}"], 1)
                dve.wait_ge(s[f"acc_free{j % 2}"], j // 2 + 1)
                dve.tensor_tensor(ga, ga, gb, ALU.add).then_inc(s["merged_sum"], 1)
                dve.wait_ge(s["mrg_hi_done"], i + 1)
                hi = mrg_hi[:, 4 * i:4 * i + 4, :].rearrange("p a b -> p (a b)").bitcast(F32)
                dve.scalar_tensor_tensor(mrg_lo[:, 4 * i:4 * i + 4, :].rearrange("p a b -> p (a b)"),
                                         ga, 0.5, hi, ALU.mult, ALU.subtract).then_inc(s["mrg_lo_done"], 1)

        def residual(i):
            j = JOB["o0"] + i
            dve.wait_ge(s["w_used"], LAST_HC[j] + 1)
            cols = xres[:, :, i * W5:(i + 1) * W5]
            dve.scalar_tensor_tensor(cols, cols, ALPHA, acc(j).rearrange("p (b n) -> p b n", b=TB),
                                     ALU.mult, ALU.add).then_inc(s[f"acc_free{j % 2}"], 1)

        def top16(vals, idx, src, spare):
            ch.step(dve.max(vals[:, 0:8], src))
            ch.wait()
            ch.step(dve.max_index(idx[:, 0:8], vals[:, 0:8], src))
            ch.step(dve.match_replace(spare, vals[:, 0:8], src, LOWEST))
            ch.wait()
            ch.step(dve.max(vals[:, 8:16], spare))
            ch.wait()
            ch.step(dve.max_index(idx[:, 8:16], vals[:, 8:16], spare))

        def pick(n):
            h, t, f = n // 6, n // 3 % TB, n % 3
            dve.wait_ge(s["sc_copied"], h // 2 + 1)
            if f < 2:
                top16(topv[:, t, h, f, :], topi[:, t, h, f, :], sc[:, h, t, f, :], sc2[:])
            else:
                ch.wait()
                c = cand[:, t, :]
                a = free(topv[:, t, h, 0, :], (1, TOPK), (0, TOPK))
                b = free(topv[:, t, h, 1, :], (0, TOPK), (1, TOPK))
                ch.step(dve.tensor_tensor(c.rearrange("p (a b) -> p a b", a=TOPK), a, b, ALU.add))
                ch.wait()
                top16(cv[:, t, h, :], cpos[:, t, h, :], c, cand2[:])

        def pre_slots(k):
            return (uT3_hi[:], uT3_lo[:]) if k % 3 == 2 else (uT_hi[:, k % 3], uT_lo[:, k % 3])

        def rest_uT(n, banks, hi, lo):
            dve.wait_ge(s["uT_hi_done"], n + 1)
            dve.tensor_tensor(lo.rearrange("p a b -> p (a b)"), ps[:, banks:banks + 2, :].rearrange("p a b -> p (a b)"),
                              hi.rearrange("p a b -> p (a b)").bitcast(F32), ALU.subtract) \
                .then_inc(s["uT_lo_done"], 1)

        def pre_split(n):
            if n < NPRE:
                rest_uT(n, 6 - 4 * (n % 2), *pre_slots(n))

        for hc in range(NHC + 2):
            if hc < NHC:
                dve.wait_ge(s["w_hi_done"], hc + 1)
                dve.tensor_tensor(w_lo[:, hc % 2], half_source(hc), w_hi[:, hc % 2].bitcast(F32),
                                  ALU.subtract).then_inc(s["w_lo_done"], 1)
            for j in range(len(JOBS)):
                if LAST_HC[j] == hc - 1:
                    if JOBS[j][0].startswith(("na", "sg")):
                        merge(j)
                    elif JOBS[j][0].startswith("o"):
                        residual(j - JOB["o0"])
            h = hc - ATT0 - 1
            if 0 <= h < HEADS:
                logits(h)
            if 0 <= h - 1 < HEADS:
                normalise(h - 1)
            if h - 4 >= 1 and (h - 4) % 2 == 1 and h - 4 < HEADS:
                yna_split((h - 4) // 2)
            if hc == HC["sv"] + 2:
                dve.wait_ge(s["acc_free%d" % (JOB["sv"] % 2)], JOB["sv"] // 2 + 1)
                layer_norm(0, sv_sb, W5, sgn_g, sgn_b, sv_sb, s["sgln_done"], s["sgn_in"])
            if hc == HC["sg"] - 1:
                gate_spatial()
            if hc == HC["sg"]:
                ysg_split()
            if hc == HC["w0"]:
                for j in (JOB["o0"], JOB["o1"]):
                    dve.wait_ge(s[f"acc_free{j % 2}"], j // 2 + 1)
                layer_norm(1, xres, D, ln1g, ln1b, xres, s["x1_ready"], s["ln1_in"])
                split_act(6, 4)
            if hc in PICKS_AT:
                for n in PICKS_AT[hc]:
                    pick(n)
        split = 0
        for n in range(PICKED, 6 * PH):
            pick(n)
            pre_split(split)
            split += 1
        ch.wait()
        cvr = cv[:].rearrange("p t h k -> p (t h) k")
        gwr = gw[:].rearrange("p t (h k) -> p (t h) k", k=TOPK)
        dve.tensor_tensor(gwr, cvr, free(cv[:, 0, 0, :], (TOPK, TB * PH), (0, TOPK)), ALU.subtract) \
            .then_inc(s["soft_in"], 1)
        flat = cpos[:].rearrange("p t h k -> p (t h k)")
        ch.step(dve.tensor_scalar(chalf[:, 0].rearrange("p t h k -> p (t h k)"), flat, 4, None,
                                  ALU.logical_shift_right))
        ch.step(dve.tensor_scalar(chalf[:, 1].rearrange("p t h k -> p (t h k)"), flat, TOPK - 1, None,
                                  ALU.bitwise_and))
        ch.step(dve.tensor_copy(topf[:].rearrange("p t h f k -> p (t h f k)"),
                                topi[:].rearrange("p t h f k -> p (t h f k)")))
        ch.wait()
        ch.step(dve.tensor_copy(chalff[:].rearrange("p f t h k -> p (f t h k)"),
                                chalf[:].rearrange("p f t h k -> p (f t h k)")))
        ch.wait()
        for t in range(TB):
            for f, dst in enumerate((e1f, e2f)):
                e = eq[:].rearrange("p (h j) a -> p h j a", h=PH)
                rank = free(chalff[:, f, t, 0, :], (1, SLOTS), (0, TOPK))
                ch.wait()
                ch.step(dve.tensor_tensor(eq[:], rank, free(iota[:, 0:1], (0, SLOTS), (1, TOPK)), ALU.is_equal))
                keys = free(topf[:, t, 0, f, :], (2 * TOPK, PH), (0, TOPK), (1, TOPK))
                pre_split(split)
                ch.wait()
                ch.step(dve.tensor_tensor(e, e, keys, ALU.mult))
                pre_split(split + 1)
                ch.wait()
                ch.step(dve.tensor_reduce(dst[:, t, :], eq[:], AX_X, ALU.add))
                pre_split(split + 2)
                split += 3
        for n in range(split, NPRE):
            pre_split(n)
        dve.wait_ge(s["soft_exp"], 1)
        ch.step(dve.tensor_reduce(gsum, gwr, AX_X, ALU.add))
        ch.wait()
        ch.step(dve.reciprocal(ginv, gsum))
        ch.wait()
        dve.tensor_tensor(gwr, gwr, free(ginv, (1, TB * PH), (0, TOPK)), ALU.mult) \
            .then_inc(s["route_done"], 1)

        dve.wait_ge(s["routeT_copied"], 3)
        G3 = G[:].rearrange("p (e t) -> p e t", t=T)

        def scale_four(group, bank, part):
            dve.wait_ge(s["g_copied"], group + 1)
            first = NB - NPRE - PB * part
            cells = G3[:, first:NB, bass.ds(4 * group, 4)]
            dve.tensor_tensor(cells, ps[:, bank, :].rearrange("p (t e) -> p e t", t=4)[:, first:NB, :], cells,
                              ALU.mult).then_inc(s["g_scaled"], 1)

        def onehots_four(group, q, first):
            if not first:
                dve.wait_ge(s["g_bank"], group - 1)
            dve.tensor_tensor(onehot2[:, 4 * q:4 * q + 4, :], free(iota[:, 0:1], (0, 4), (1, NK)),
                              e2T[:, bass.ds(4 * group, 4)].unsqueeze(2).broadcast_to([P, 4, NK]), ALU.is_equal)
            for k in range(4):
                ins = dve.tensor_scalar(onehot1g[:, 4 * q + k, :], iota[:], e1T[:, bass.ds(4 * group + k, 1)],
                                        gT[:, bass.ds(4 * group + k, 1)], ALU.is_equal, ALU.mult)
            ins.then_inc(s["onehots"], 1)

        def during(part, i, slot, head):
            h = PB * part + 2 * i + slot
            for q in range(2):
                onehots_four(2 * h + q, q, head)
            rest_uT(NPRE + h + 1, 6, uT_hi[:, 1 - slot], uT_lo[:, 1 - slot])
            for q in range(2):
                if not (head or (isinstance(i, int) and i == 0 and slot == 0)):
                    scale_four(2 * h + q - 2, 2 * (1 - slot) + q, part)

        rest_uT(NPRE, 6, uT_hi[:, 0], uT_lo[:, 0])
        for part in range(PARTS):
            for slot in range(2):
                during(part, 0, slot, part == 0 and slot == 0)
            with dve.Fori(1, PB // 2) as i:
                for slot in range(2):
                    during(part, i, slot, False)
            for q in range(2):
                scale_four(2 * (PB * (part + 1) - 1) + q, 2 + q, part)
            top = NB - NPRE - PB * part
            dve.wait_ge(s["act_done"], NPRE + PB * (part + 1))
            cells = G3[:, top - PB:top, 0:PT * (part + 1)]
            dve.tensor_tensor(cells, cells, early[:, :, 0:PT * (part + 1)], ALU.mult) \
                .then_inc(s["settled_mult"], 1)
            dve.wait_ge(s["settled_mult"], part + 1)
            if part < PARTS - 1:
                dve.wait_ge(s["settled_copy"], part + 1)

        def rest_v(n, slot):
            for d in range(2):
                dve.wait_ge(s["v_hi_done"], 2 * n + d + 1)
                dve.tensor_tensor(v_lo[:, slot, d * 512:(d + 1) * 512], v_raw[:, slot, d * 512:(d + 1) * 512],
                                  v_hi[:, slot, d * 512:(d + 1) * 512].bitcast(F32),
                                  ALU.subtract).then_inc(s["v_lo_done"], 1)

        def split_hidden(n, slot, hidden, head):
            if not head:
                dve.wait_ge(s["y_done"], n - 1)
            dve.tensor_copy(hid_hi[:, slot, :], hidden).then_inc(s["hid_h"], 1)
            dve.wait_ge(s["hid_h"], n + 1)
            dve.tensor_tensor(hid_lo[:, slot, :], hidden, hid_hi[:, slot, :].bitcast(F32),
                              ALU.subtract).then_inc(s["hid_done"], 1)

        for slot in range(2):
            split_hidden(slot, slot, G[:, (NB - NEARLY + slot) * T:(NB - NEARLY + slot + 1) * T], True)
            rest_v(slot, slot)
        with dve.Fori(1, NEARLY // 2) as i:
            for slot in range(2):
                split_hidden(2 * i + slot, slot, G[:, bass.ds((2 * i + (NB - NEARLY + slot)) * T, T)], False)
                rest_v(2 * i + slot, slot)
        rest_v(NEARLY, 0)

        def pair(j, tail):
            for slot in range(2):
                n = 2 * j + (NEARLY + slot)
                dve.wait_ge(s["act_done"], n + 1)
                dve.tensor_tensor(act_e[:, slot, :], act_e[:, slot, :], G[:, bass.ds((2 * j + slot) * T, T)], ALU.mult) \
                    .then_inc(s["hid_m"], 1)
                dve.wait_ge(s["hid_m"], n - NEARLY + 1)
                split_hidden(n, slot, act_e[:, slot, :], False)
                if tail and slot == 1:
                    continue
                rest_uT(n + 1, 6, uT_hi[:, 1 - slot], uT_lo[:, 1 - slot])
                rest_v(n + 1, 1 - slot)

        with dve.Fori(0, (NB - NEARLY) // 2 - 1) as j:
            pair(j, False)
        pair((NB - NEARLY) // 2 - 1, True)
        dve.wait_ge(s["y_done"], NB)
        for t in range(TB):
            ch.step(dve.scalar_tensor_tensor(xres[:, t, :], xres[:, t, :], ALPHA,
                                             ps[:, 2 * t:2 * t + 2, :].rearrange("p a b -> p (a b)"),
                                             ALU.mult, ALU.add))
        layer_norm(2, xres, D, ln2g, ln2b, xres, s["out_ready"], s["ln2_in"])

    @block.tensor
    def _(pe):
        pe.wait_ge(s["ident_ready"], 3)

        def transpose_rows(ready, wait_free):
            for t, g in ((t, g) for g in range(4) for t in range(TB)):
                if t == 0:
                    wait_free(g)
                    pe.wait_ge(*ready)
                for k in range(2):
                    ins = pe.transpose(ps[:, 4 + g, k * T + t * P:k * T + (t + 1) * P],
                                       xres[:, t, (2 * g + k) * P:(2 * g + k + 1) * P], ident[:])
                if t == TB - 1:
                    ins.then_inc(s["tp_done"], 1)

        transpose_rows((s["x_in"], 16), lambda g: None)
        pe.wait_ge(s["ws_in"], 16)
        pe.wait_ge(s["act_lo_done"], 1)
        for g in range(GROUPS):
            ins = pe.transpose(ps[:, 4, g * P:(g + 1) * P], ws_raw[:, g, :], ident[:])
        ins.then_inc(s["tp_done"], 1)
        pe.wait_ge(s["sk_in"], 32)
        pe.wait_ge(s["act_lo_done"], 2)
        for f in range(2):
            ins = pe.transpose(ps[:, 5, f * P:(f + 1) * P], sk_raw[:, f, :], ident[:])
        ins.then_inc(s["tp_done"], 1)

        def scores(h):
            pe.wait_ge(s["acc_free1"], 1)
            if h == 0:
                pe.wait_ge(s["tp_copied"], 2)
            else:
                pe.wait_ge(s["logit_done"], h)
            p0 = DH * (h % 2)
            for b in range(TB):
                ins = pe.matmul(ps[:, 4, b * T:(b + 1) * T], qT[p0:p0 + DH, h // 2, b * P:(b + 1) * P],
                                kT[p0:p0 + DH, h // 2, :], start=True, stop=True)
            ins.then_inc(s["score_done"], 1)

        def transpose_probs(h):
            pe.wait_ge(s["prob_ready"], 2 * h + 2)
            if h >= 1:
                pe.wait_ge(s["probT_copied"], h)
            for kb in range(TB):
                for b in range(TB):
                    ins = pe.transpose(ps[:, 5, kb * T + b * P:kb * T + (b + 1) * P],
                                       prob[:, h % 2, b, kb * P:(kb + 1) * P], ident[:])
            ins.then_inc(s["probT_done"], 1)

        def times_v(h):
            pe.wait_ge(s["probT_copied"], h + 1)
            pe.wait_ge(s["acc_free0"], 2)
            if h >= 2 and h % 2 == 0:
                pe.wait_ge(s["yna_lo_done"], h // 2)
            p0 = DH * (h % 2)
            for kb in range(TB):
                ins = pe.matmul(ps[p0:p0 + DH, 6, 0:T], v_sb[:, kb, h * DH:(h + 1) * DH], probT[:, h % 2, kb, :],
                                start=(kb == 0), stop=(kb == TB - 1))
            ins.then_inc(s["pv_done"], 1)

        def mix():
            pe.wait_ge(s["yna_lo_done"], HEADS // 2)
            for b in range(TB):
                pe.wait_ge(s["sgln_done"], b + 1)
                for g in range(GROUPS):
                    ins = pe.matmul(ps[:, 6 + b, g * P:(g + 1) * P], wsT[:, g, :], sv_sb[:, b, g * P:(g + 1) * P],
                                    start=True, stop=True)
                ins.then_inc(s["mix_done"], 1)

        def transpose_ysg():
            pe.wait_ge(s["logit_done"], HEADS)
            pe.wait_ge(s["probT_copied"], HEADS)
            pe.wait_ge(s["ysg_done"], TB * GROUPS)
            for b2 in range(2):
                for k in range(2):
                    for t in range(TB):
                        g = 2 * b2 + k
                        ins = pe.transpose(ps[:, 4 + b2, k * T + t * P:k * T + (t + 1) * P],
                                           ysg[:, t, g * P:(g + 1) * P], ident[:])
                ins.then_inc(s["ysgT_done"], 1)

        def key_scores(i):
            j = JOB["w0"] + i
            pe.wait_ge(s[f"acc_free{j % 2}"], j // 2 + 1)
            if i == 0:
                pe.wait_ge(s["act_lo_done"], 8)
            else:
                pe.wait_ge(s["sc_copied"], i)
            for hh in range(2):
                for t in range(TB):
                    for f in range(2):
                        c = (t * 2 + f) * NK
                        ins = pe.matmul(ps[:, 4 + hh, c:c + NK], pqT[:, i % 2, 2 * hh + f, t * P:(t + 1) * P],
                                        skT[:, f, :], start=True, stop=True)
            ins.then_inc(s["key_scores"], 1)

        for hc in range(NHC + 2):
            if hc < NHC:
                j = JOB_OF_HC[hc]
                name, hcs = JOBS[j]
                first = hc == hcs[0]
                if first and j >= 2:
                    pe.wait_ge(s[f"acc_free{j % 2}"], j // 2)
                if name in ("na0", "sg0"):
                    n = {"na0": ("yna_lo_done", HEADS // 2), "sg0": ("ysgT_lo_done", 2)}[name]
                    pe.wait_ge(s[n[0]], n[1])
                if name == "o0" and first:
                    pe.wait_ge(s["mrg_lo_done"], 1)
                if name == "o0" and not first:
                    pe.wait_ge(s["mrg_lo_done"], 2)
                if name == "q" and first:
                    pe.wait_ge(s["act_lo_done"], 4)
                if name == "w0" and first:
                    pe.wait_ge(s["act_lo_done"], 8)
                pe.wait_ge(s["w_lo_done"], hc + 1)
                a_hi, a_lo = {"n": (yna_hi, yna_lo), "s": (act_hi, act_lo), "o": (mrg_hi, mrg_lo)} \
                    .get(name[0], (act_hi, act_lo))
                if name in ("sg0", "sg1"):
                    a_hi, a_lo = ysgT_hi, ysgT_lo
                k0 = KW * hcs.index(hc)
                natural = name in ("v", "sv", "su", "o0", "o1")
                a = acc(j)
                slot = hc % 2
                for m in range(TB if natural else 4):
                    for k in range(KW):
                        for part in range(3):
                            ah = (a_hi, a_lo, a_hi)[part]
                            wh = (w_hi, w_hi, w_lo)[part]
                            if natural:
                                dst = a[:, m * W5:(m + 1) * W5]
                                l = ah[:, k0 + k, m * P:(m + 1) * P]
                                r = wh[:, slot, k, :]
                                opens = first and k == 0 and part == 0
                            else:
                                dst = a[:, m * T:(m + 1) * T]
                                l = wh[:, slot, k, m * P:(m + 1) * P]
                                r = ah[:, k0 + k, :]
                                opens = first and k == 0 and part == 0 and m % 2 == 0
                            ins = pe.matmul(dst, l, r, start=opens, stop=(hc == hcs[-1] and k == KW - 1 and part == 2),
                                            skip_group_check=True)
                ins.then_inc(s["w_used"], 1)
            h = hc - ATT0
            if 0 <= h < HEADS:
                scores(h)
            if 0 <= h - 2 < HEADS:
                transpose_probs(h - 2)
            if 0 <= h - 4 < HEADS:
                times_v(h - 4)
            if hc == HC["na"]:
                mix()
            if hc == HC["sg"] - 1:
                transpose_ysg()
            if hc == HC["o1"] + 1:
                def free_bank(g):
                    pe.wait_ge(s["ysgT_lo_done"], 2)
                    pe.wait_ge(s["ysg_done"], TB * GROUPS)
                for t in range(TB):
                    pe.wait_ge(s["x1_ready"], t + 1)
                transpose_rows((s["x1_ready"], TB), free_bank)
            if hc >= HC["w0"] + 2 and (hc - HC["w0"] - 2) % 2 == 0 and (hc - HC["w0"] - 2) // 2 < 4:
                key_scores((hc - HC["w0"] - 2) // 2)

        def transpose_u(landed, slot, banks):
            pe.wait_ge(s[f"u_in{slot}"], landed)
            for k in range(KD):
                ins = pe.transpose(ps[:, banks + k // 4, (k % 4) * P:(k % 4 + 1) * P],
                                   u_raw[:, slot, k * P:(k + 1) * P], ident[:])
            ins.then_inc(s["u_read"], 1)

        def expert_inputs(hi, lo, bank):
            for k in range(KD):
                for part in range(3):
                    ins = pe.matmul(ps[:, bank, 0:T], (hi, hi, lo)[part][:, k, :],
                                    (act_hi, act_lo, act_hi)[part][:, k, :],
                                    start=(k == 0 and part == 0), stop=(k == KD - 1 and part == 2))
            ins.then_inc(s["a_done"], 1)

        def pre_slots(k):
            return (uT3_hi[:], uT3_lo[:]) if k % 3 == 2 else (uT_hi[:, k % 3], uT_lo[:, k % 3])

        def pre_six(i, head, last):
            for k in range(6):
                n = 6 * i + k
                pe.wait_ge(s["uT_lo_done"], n + 1)
                if not (last and k >= 4):
                    transpose_u(48 * i + 16 * ((k + 2) // 2 + 1), k % 2, 6 - 4 * (k % 2))
                if not (head and k < 2):
                    pe.wait_ge(s["act_done"], n - 1)
                expert_inputs(*pre_slots(k), k % 2)

        pe.wait_ge(s["sc_copied"], 4)
        transpose_u(16, 0, 6)
        transpose_u(16, 1, 2)
        pre_six(0, True, False)
        with pe.Fori(1, NPRE // 6 - 1) as i:
            pre_six(i, False, False)
        pre_six(NPRE // 6 - 1, False, True)
        pe.wait_ge(s["act_done"], NPRE)
        pe.wait_ge(s["route_done"], 1)
        for n, src in enumerate((e1f, e2f, gw)):
            for t in range(TB):
                ins = pe.transpose(ps[:, 4 + n, t * P:(t + 1) * P], src[:, t, :], ident[:])
        ins.then_inc(s["routeT_done"], 1)
        def during(part, i, slot, head):
            h = PB * part + 2 * i + slot
            n = NPRE + h
            pe.wait_ge(s["uT_lo_done"], n + 1)
            transpose_u(8 * (NPRE + PB * part) + 16 * i + 16 + 16 * slot, 1 - slot, 6)
            pe.wait_ge(s["act_done"], n - 1)
            expert_inputs(uT_hi[:, slot], uT_lo[:, slot], 4 + slot)
            for q in range(2):
                pe.wait_ge(s["onehots"], 2 * h + q + 1)
                if not head:
                    pe.wait_ge(s["g_copied"], 2 * h + q - 3)
                    pe.wait_ge(s["g_scaled"], 2 * h + q - 3)
                for k in range(4):
                    ins = pe.matmul(ps[:, 2 * slot + q, k * NK:(k + 1) * NK], onehot2[:, 4 * q + k, :],
                                    onehot1g[:, 4 * q + k, :], start=True, stop=True)
                ins.then_inc(s["g_bank"], 1)

        pe.wait_ge(s["routeT_copied"], 3)
        transpose_u(8 * NPRE + 16, 0, 6)
        for part in range(PARTS):
            if part == 0:
                for slot in range(2):
                    during(0, 0, slot, True)
            with pe.Fori(1 if part == 0 else 0, PB // 2) as i:
                for slot in range(2):
                    during(part, i, slot, False)

        def expert_outputs(slot, opens, closes):
            for t in range(TB):
                for part in range(3):
                    h = (hid_hi, hid_lo, hid_hi)[part][:, slot, t * P:(t + 1) * P]
                    v = (v_hi, v_hi, v_lo)[part]
                    for d in range(2):
                        ins = pe.matmul(ps[:, 2 * t + d, :], h, v[:, slot, d * 512:(d + 1) * 512],
                                        start=(opens and part == 0), stop=(closes and part == 2),
                                        skip_group_check=True)
            ins.then_inc(s["y_done"], 1)

        pe.wait_ge(s["g_copied"], T // 4)
        pe.wait_ge(s["g_scaled"], T // 4)

        def outputs_of(n, slot, opens, closes):
            pe.wait_ge(s["hid_done"], n + 1)
            pe.wait_ge(s["v_lo_done"], 2 * n + 2)
            expert_outputs(slot, opens, closes)

        outputs_of(0, 0, True, False)
        outputs_of(1, 1, False, False)
        with pe.Fori(1, NEARLY // 2) as i:
            for slot in range(2):
                outputs_of(2 * i + slot, slot, False, False)

        def pair(i, head, tail):
            for slot in range(2):
                n = 2 * i + slot
                pe.wait_ge(s["uT_lo_done"], n + 1)
                if not head:
                    pe.wait_ge(s["act_done"], n - 1)
                expert_inputs(uT_hi[:, slot], uT_lo[:, slot], 4 + slot)
                if not (tail and slot == 1):
                    transpose_u(16 * i + 16 if slot == 0 else 16 * i + 32, 1 - slot, 6)
                if not (head and slot == 0):
                    outputs_of(n - 1, 1 - slot, False, False)

        pair(NEARLY // 2, True, False)
        with pe.Fori(NEARLY // 2 + 1, NB // 2 - 1) as i:
            pair(i, False, False)
        pair(NB // 2 - 1, False, True)
        outputs_of(NB - 1, 1, False, True)

    blocks.__exit__(None, None, None)


_INS = ["x", "w_in", "na_rpb", "sg_norm_g", "sg_norm_b", "sg_spatial_w", "sg_spatial_b", "w_branch_na",
        "w_branch_sg", "w_out", "ln1_g", "ln1_b", "peer_wq", "peer_subkeys1", "peer_subkeys2", "peer_u",
        "peer_v", "ln2_g", "ln2_b"]
_OUTS = [((1, T, D), "float32")]


def kernel(**inputs):
    import numpy as _np
    import concourse.bacc as _bacc
    from concourse import mybir as _mybir
    from concourse.bass_utils import run_bass_kernel_spmd as _run

    nc = _bacc.Bacc("TRN2", target_bir_lowering=False, num_devices=1)
    arrays, args = {}, []
    for name in _INS:
        a = inputs[name]
        if name == "na_rpb":
            a = _np.asarray(a)[:, :, ::-1, ::-1]
        a = _np.ascontiguousarray(a)
        arrays[f"in_{name}_dram"] = a
        args.append(nc.dram_tensor(f"in_{name}_dram", a.shape, _mybir.dt.from_np(a.dtype), kind="ExternalInput").ap())
    for i, (shape, dtype) in enumerate(_OUTS):
        dt = _mybir.dt.from_np(_np.dtype(dtype))
        args.append(nc.dram_tensor(f"out_{i}_dram", shape, dt, kind="ExternalOutput").ap())
    hybrid_block(nc, *args)
    r = _run(nc, [arrays], core_ids=[0])
    got = tuple(r.results[0][f"out_{i}_dram"] for i in range(len(_OUTS)))
    return got[0]
```

```python
import math

import concourse.bass as bass
from concourse import mybir

F32 = mybir.dt.float32
F32R = mybir.dt.float32r
U32 = mybir.dt.uint32
ALU = mybir.AluOpType
ACT = mybir.ActivationFunctionType
AX_X = mybir.AxisListType.X

P = 128
D = 1024
T = 256
TB = T // P
KD = D // P
HEADS, DH = 8, 64
GRID_W, ROWS = 64, T // 64
WIN_H, WIN_W = 8, 16
RPB_W = 2 * WIN_W - 1
RPB_H = 2 * WIN_H - 1
W5 = 512
KW = W5 // P
GROUPS = 4
PH = 8
NK = 128
TOPK = 16
SLOTS = PH * TOPK
NEXP = NK * NK
ALPHA = 2.0 ** 0.25
EPS = 1e-5
LOWEST = -3.0e38
MASKED = -1.0e30
NB = NK
NPRE = 42
NDUR = 32
NEARLY = NPRE + NDUR
V_BEFORE = 16 * -(-NEARLY // 4)
BODY = 8
PARTS = 4
PT = T // PARTS
PB = NDUR // PARTS

CHUNKS = ["q", "k", "v", "sv", "su", "ga0", "ga1", "gb0", "gb1", "sg", "na", "o0", "o1", "w0", "w1", "w2", "w3"]
COL0 = {"q": 0, "k": W5, "v": 2 * W5, "su": 3 * W5, "sv": 4 * W5,
        "ga0": 5 * W5, "ga1": 6 * W5, "gb0": 7 * W5, "gb1": 8 * W5}
NHC = 2 * len(CHUNKS)
JOBS = []
for _c, _n in enumerate(CHUNKS):
    if _n in ("na", "sg"):
        JOBS += [(_n + "0", [2 * _c]), (_n + "1", [2 * _c + 1])]
    else:
        JOBS.append((_n, [2 * _c, 2 * _c + 1]))
JOB = {n: j for j, (n, _) in enumerate(JOBS)}
JOB_OF_HC = {h: j for j, (_, hs) in enumerate(JOBS) for h in hs}
LAST_HC = {j: hs[-1] for j, (_, hs) in enumerate(JOBS)}
HC = {n: 2 * c for c, n in enumerate(CHUNKS)}
BIAS_HEADS = ((0, 2), (2, 5), (5, HEADS))
ATT0 = HC["v"] + 2

MIX0 = HC["sv"] + 5
YSGT0 = MIX0 + 3


PICKS_AT = {HC["w2"]: [0, 1], HC["w2"] + 1: [2, 3], HC["w3"]: [4, 5, 6], HC["w3"] + 1: [7, 8, 9]}
PICKED = 10
STEPS = 6 * PH - PICKED + 3 * 2 * TB


Q = 32
NQ = P // Q


def free(ap, *dims, start=0):
    return bass.AP(ap.tensor, ap.offset + start, [list(ap.ap[0]), *[list(d) for d in dims]])


def hybrid_block(nc, x, w_in, na_rpb, sg_norm_g, sg_norm_b, sg_spatial_w, sg_spatial_b, w_branch_na,
                 w_branch_sg, w_out, ln1_g, ln1_b, peer_wq, peer_subkeys1, peer_subkeys2, peer_u,
                 peer_v, ln2_g, ln2_b, out):
    K1 = 1024
    base = 16512

    def sb(name, shape, at, dt=F32):
        return nc.alloc_sbuf_tensor_at(name, shape, dt, offset=base + int(at))

    ident = sb("ident", [P, P], 0)
    iota = sb("iota", [P, P], 512)
    act_hi = sb("act_hi", [P, KD, T], 1 * K1, F32R)
    act_lo = sb("act_lo", [P, KD, T], 9 * K1, F32R)
    xres = sb("xres", [P, TB, D], 17 * K1)
    w_raw = sb("w_raw", [P, 2, 2 * KW * W5], 25 * K1)
    w_hi = sb("w_hi", [P, 2, KW, W5], 57 * K1, F32R)
    w_lo = sb("w_lo", [P, 2, KW, W5], 73 * K1, F32R)
    qT = sb("qT", [P, KW, T], 89 * K1)
    kT = sb("kT", [P, KW, T], 93 * K1)
    v_sb = sb("v_sb", [P, TB, W5], 97 * K1)
    sv_sb = sb("sv_sb", [P, TB, W5], 101 * K1)
    su_sb = sb("su_sb", [P, TB, W5], 105 * K1)
    ysg = sb("ysg", [P, TB, W5], 109 * K1)
    ws_raw = sb("ws_raw", [P, GROUPS, P], 113 * K1)
    wsT = sb("wsT", [P, GROUPS, P], 115 * K1)
    sgn_g = sb("sgn_g", [P, W5], 117 * K1)
    sgn_b = sb("sgn_b", [P, W5], 119 * K1)
    bias = sb("bias", [P, HEADS, TB, T], 121 * K1)
    mrg_hi = sb("mrg_hi", [P, KD, T], 121 * K1, F32R)
    mrg_lo = sb("mrg_lo", [P, KD, T], 129 * K1, F32R)
    prob = sb("prob", [P, 2, TB, T], 137 * K1)
    probT = sb("probT", [P, 2, TB, T], 141 * K1)
    yna_hi = sb("yna_hi", [P, KW, T], 145 * K1, F32R)
    yna_lo = sb("yna_lo", [P, KW, T], 149 * K1, F32R)
    ysgT_hi = sb("ysgT_hi", [P, KW, T], 153 * K1, F32R)
    ysgT_lo = sb("ysgT_lo", [P, KW, T], 157 * K1, F32R)
    gates = sb("gates", [P, 2 * KD, T], 161 * K1)
    ln1g = sb("ln1g", [P, D], 177 * K1)
    ln1b = sb("ln1b", [P, D], 181 * K1)
    sk_raw = sb("sk_raw", [P, 2, P], 185 * K1)
    skT = sb("skT", [P, 2, P], 186 * K1)
    pqT = sb("pqT", [P, 2, KW, T], 161 * K1)
    sc = sb("sc", [P, PH, TB, 2, NK], 89 * K1)
    eq = sb("eq", [P, SLOTS, TOPK], 25 * K1)
    e1f = sb("e1f", [P, TB, SLOTS], 187 * K1)
    e2f = sb("e2f", [P, TB, SLOTS], 188 * K1)
    gw = sb("gw", [P, TB, SLOTS], 189 * K1)
    topv = sb("topv", [P, TB, PH, 2, TOPK], 190 * K1)
    topi = sb("topi", [P, TB, PH, 2, TOPK], 192 * K1, U32)
    topf = sb("topf", [P, TB, PH, 2, TOPK], 194 * K1)
    cand = sb("cand", [P, 2, TOPK * TOPK], 196 * K1)
    cand2 = sb("cand2", [P, TOPK * TOPK], 198 * K1)
    sc2 = sb("sc2", [P, NK], 199 * K1)
    cv = sb("cv", [P, TB, PH, TOPK], 200 * K1)
    cpos = sb("cpos", [P, TB, PH, TOPK], 201 * K1, U32)
    chalf = sb("chalf", [P, 2, TB, PH, TOPK], 202 * K1, U32)
    chalff = sb("chalff", [P, 2, TB, PH, TOPK], 204 * K1)
    G = sb("G", [P, NK * T], 25 * K1)
    onehot2 = sb("onehot2", [P, 8, NK], 193 * K1)
    onehot1g = sb("onehot1g", [P, 8, NK], 197 * K1)
    e1T = sb("e1T", [P, T], 204 * K1)
    e2T = sb("e2T", [P, T], 205 * K1)
    gT = sb("gT", [P, T], 206 * K1)
    early = sb("early", [P, PB, T], 185 * K1)
    u_raw = sb("u_raw", [P, 2, D], 153 * K1)
    v_raw = sb("v_raw", [P, 2, D], 161 * K1)
    uT_hi = sb("uT_hi", [P, 2, KD, P], 169 * K1, F32R)
    uT_lo = sb("uT_lo", [P, 2, KD, P], 177 * K1, F32R)
    uT_raw = sb("uT_raw", [P, 2, KD, P], 177 * K1)
    uT3_hi = sb("uT3_hi", [P, KD, P], 161 * K1, F32R)
    uT3_lo = sb("uT3_lo", [P, KD, P], 165 * K1, F32R)
    v_hi = sb("v_hi", [P, 2, D], 185 * K1, F32R)
    v_lo = sb("v_lo", [P, 2, D], 193 * K1, F32R)
    act_e = sb("act_e", [P, 2, T], 201 * K1)
    hid_hi = sb("hid_hi", [P, 2, T], 203 * K1, F32R)
    hid_lo = sb("hid_lo", [P, 2, T], 205 * K1, F32R)
    ln2g = sb("ln2g", [P, D], 25 * K1)
    ln2b = sb("ln2b", [P, D], 29 * K1)
    small = sb("small", [P, 84], 207 * K1)
    stats = small[:, 0:24]
    mv = small[:, 24:28]
    rstd = small[:, 28:30]
    rmax = small[:, 32:36]
    rsum = small[:, 36:40]
    rinv = small[:, 40:44]
    eps = small[:, 44:45]
    bsT = small[:, 48:52]
    gsum = small[:, 52:68]
    ginv = small[:, 68:84]

    ps = nc.psum_tensor("ps", [P, 8, 512], F32).__enter__()

    def acc(j):
        return ps[:, 2 * (j % 2):2 * (j % 2) + 2, :].rearrange("p a b -> p (a b)")

    names = ["x_in", "rpb_in0", "rpb_in1", "rpb_in2", "ws_in", "bs_in", "sgn_in", "ln1_in", "sk_in", "ln2_in",
             "w_first", "w_in0", "w_in1", "w_hi_done", "w_lo_done", "w_used", "o1_first", "residual", "acc_free0", "acc_free1",
             "pool_done", "mask_done", "ident_ready", "tp_done", "tp_hi", "tp_lo", "tp_copied", "score_done", "logit_done",
             "max_done", "exp_done", "prob_ready", "probT_done", "probT_copied", "pv_done", "yna_hi_done",
             "yna_lo_done", "gelu_done", "mix_done", "sgln_done", "ysg_done", "ysgT_done", "ysgT_hi_done",
             "ysgT_lo_done", "merged_sum", "mrg_hi_done", "mrg_lo_done", "ln_var", "ln_std", "x1_ready",
             "act_hi_done", "act_lo_done", "key_scores", "sc_copied", "soft_in", "soft_exp", "route_done",
             "routeT_done", "routeT_copied", "onehots", "g_bank", "g_copied", "g_scaled", "settled_mult", "settled_copy",
             "u_in0", "u_in1", "v_in0", "v_in1", "v_in2", "v_in3", "u_read", "u_turned", "uT_hi_done", "uT_lo_done", "v_hi_done",
             "v_lo_done", "a_done", "act_done", "hid_done", "hid_m", "hid_h", "y_first", "y_done", "z_done", "out_ready",
             "stored", "dve"]
    s = {n: nc.semaphore(n).__enter__() for n in names}

    class Chain:

        def __init__(self, eng, sem):
            self.eng, self.sem, self.n = eng, sem, 0

        def step(self, ins):
            ins.then_inc(self.sem, 1)
            self.n += 1
            return self.n

        def wait(self, n=None):
            self.eng.wait_ge(self.sem, self.n if n is None else n)

    u_dram = peer_u[0]
    v_dram = peer_v[0]

    def chunk_source(n):
        if n in COL0:
            return w_in[0, :, COL0[n]:COL0[n] + W5].rearrange("(p k) n -> p k n", p=P)
        if n in ("na", "sg"):
            w = w_branch_na if n == "na" else w_branch_sg
            return w[0].rearrange("(k p) n -> p k n", p=P)
        c = int(n[1]) * W5
        if n[0] == "w":
            return peer_wq[0, :, c:c + W5].rearrange("(p k) n -> p k n", p=P)
        return w_out[0, :, c:c + W5].rearrange("(k p) n -> p k n", p=P)

    def v_slot(m):
        return v_raw[:, m % 4, :] if m % 4 < 2 else u_raw[:, m % 4 - 2, :]

    def half_source(hc):
        c = hc // 2
        raw = w_raw[:, c % 2, :]
        if CHUNKS[c] in ("na", "sg"):
            return raw.rearrange("p (k n) -> p k n", k=KW)[:, :, (hc % 2) * W5:(hc % 2 + 1) * W5]
        return raw.rearrange("p (k n) -> p k n", k=KD)[:, (hc % 2) * KW:(hc % 2 + 1) * KW, :]

    blocks = nc.Block()
    block = blocks.__enter__()

    @block.sync
    def _(sp):
        def load_bias(group):
            for h in range(*BIAS_HEADS[group]):
                for r in range(ROWS):
                    at = (h * RPB_H + WIN_H - ROWS + r) * RPB_W + WIN_W - GRID_W
                    src = bass.AP(na_rpb.tensor, na_rpb.offset + at,
                                  [[1, GRID_W], [RPB_W, ROWS], [1, GRID_W]])
                    b, p0 = r // 2, GRID_W * (r % 2)
                    dst = bias[p0:p0 + GRID_W, h, b, :].rearrange("p (r c) -> p r c", r=ROWS)
                    sp.dma_start(dst, src).then_inc(s[f"rpb_in{group}"], 16)

        sp.dma_start(xres[:], x[0].rearrange("(b p) d -> p b d", p=P)).then_inc(s["x_in"], 16)
        for c, n in enumerate(CHUNKS):
            if c >= 2:
                sp.wait_ge(s["w_lo_done"], 2 * (c - 1))
            dst = w_raw[:, c % 2, :].rearrange("p (k n) -> p k n", k=KW if n in ("na", "sg") else KD)
            if c == 0:
                sp.dma_start(dst[:, 0:KW, :], chunk_source(n)[:, 0:KW, :]).then_inc(s["w_first"], 16)
                sp.dma_start(dst[:, KW:KD, :], chunk_source(n)[:, KW:KD, :]).then_inc(s["w_in0"], 16)
            else:
                sp.dma_start(dst, chunk_source(n)).then_inc(s[f"w_in{c % 2}"], 16)
            if c == 0:
                sp.dma_start(ws_raw[:], sg_spatial_w[0].rearrange("g p q -> p g q")).then_inc(s["ws_in"], 16)
                sp.dma_start(sk_raw[:, 0, :], peer_subkeys1[0]).then_inc(s["sk_in"], 16)
                sp.dma_start(sk_raw[:, 1, :], peer_subkeys2[0]).then_inc(s["sk_in"], 16)
            if 1 <= c <= len(BIAS_HEADS):
                load_bias(c - 1)
            if c == 2:
                sp.dma_start(bsT, sg_spatial_b[0].rearrange("g p -> p g"),
                             allow_slow_non_contiguous=True).then_inc(s["bs_in"], 16)
                sp.dma_start(sgn_g[:], sg_norm_g[0:1, :].broadcast_to([P, W5])).then_inc(s["sgn_in"], 16)
                sp.dma_start(sgn_b[:], sg_norm_b[0:1, :].broadcast_to([P, W5])).then_inc(s["sgn_in"], 16)
            if c == 5:
                sp.dma_start(ln1g[:], ln1_g[0:1, :].broadcast_to([P, D])).then_inc(s["ln1_in"], 16)
                sp.dma_start(ln1b[:], ln1_b[0:1, :].broadcast_to([P, D])).then_inc(s["ln1_in"], 16)

        def load_u(b, slot):
            sp.dma_start(u_raw[:, slot, :], u_dram[bass.ds(b * P, P), :]).then_inc(s[f"u_in{slot}"], 16)

        def load_u_squares(b, slot):
            rows = u_dram[bass.ds(b * P, P), :].rearrange("(c i) (a m) -> a i c m", c=NQ, a=NQ)
            for a in range(NQ):
                sp.dma_start(u_raw[a * Q:(a + 1) * Q, slot, :].rearrange("p (c m) -> p c m", c=NQ), rows[a]) \
                    .then_inc(s[f"u_in{slot}"], 16)

        def load_v(b, slot):
            sp.dma_start(v_raw[:, slot, :], v_dram[bass.ds(b * P, P), :]).then_inc(s[f"v_in{slot}"], 16)

        sp.wait_ge(s["mrg_lo_done"], 2)
        for slot in range(2):
            load_u(NB - NPRE + slot, slot)
        with sp.Fori(1, NPRE // 2) as i:
            for slot in range(2):
                sp.wait_ge(s["u_read"], 2 * i + slot - 1)
                load_u(2 * i + (NB - NPRE + slot), slot)
        for slot in range(2):
            sp.wait_ge(s["u_read"], NPRE + slot - 1)
            load_u(NB - NPRE - PB + slot, slot)
        sp.wait_ge(s["a_done"], NPRE)
        for slot in range(2):
            load_v(NB - NPRE + slot, slot)
        for part in range(PARTS):
            with sp.Fori(0 if part else 1, PB // 2) as i:
                for slot in range(2):
                    sp.wait_ge(s["u_read"], 2 * i + (NPRE + PB * part + slot - 1))
                    load_u(2 * i + (NB - NPRE - PB * (part + 1) + slot), slot)
        sp.wait_ge(s["u_read"], NEARLY - 1)
        load_u(0, 0)
        sp.wait_ge(s["u_read"], NEARLY)
        load_u_squares(1, 1)

        def load_early_v(b, k):
            sp.dma_start(v_slot(k), v_dram[bass.ds(b * P, P), :]).then_inc(s[f"v_in{k % 4}"], 16)

        sp.wait_ge(s["u_read"], NEARLY + 1)
        load_early_v(NB - NPRE + 2, 2)
        sp.wait_ge(s["u_turned"], 1)
        load_early_v(NB - NPRE + 3, 3)
        for m in range(4, 6):
            sp.wait_ge(s["v_lo_done"], 2 * (m - 3))
            load_early_v(NB - NPRE + m, m)
        with sp.Fori(0, (NPRE - 6) // 4) as i:
            for k in range(4):
                sp.wait_ge(s["v_lo_done"], 8 * i + 2 * (3 + k))
                load_early_v(4 * i + (NB - NPRE + 6 + k), 6 + k)
        with sp.Fori(0, NDUR // 4) as i:
            for k in range(4):
                sp.wait_ge(s["v_lo_done"], 8 * i + 2 * (NPRE - 3 + k))
                load_early_v(4 * i + (NB - NEARLY + k), NPRE + k)
        for slot in range(2):
            sp.wait_ge(s["v_lo_done"], 2 * (NEARLY - 3 + slot))
            load_u_squares(2 + slot, slot)
        for slot in range(2):
            sp.wait_ge(s["v_lo_done"], 2 * (NEARLY + slot - 1))
            load_v(slot, slot)
        with sp.Fori(1, (NB - NEARLY) // 2 - 1) as i:
            for slot in range(2):
                sp.wait_ge(s["u_turned"], 2 * i + slot)
                load_u_squares(2 * i + (2 + slot), slot)
                sp.wait_ge(s["v_lo_done"], 4 * i + 2 * (NEARLY + slot - 1))
                load_v(2 * i + slot, slot)
        for slot in range(2):
            sp.wait_ge(s["v_lo_done"], 2 * (NB + slot - 3))
            load_v(NB - NEARLY - 2 + slot, slot)
        sp.wait_ge(s["hid_h"], NB)
        sp.dma_start(ln2g[:], ln2_g[0:1, :].broadcast_to([P, D])).then_inc(s["ln2_in"], 16)
        sp.dma_start(ln2b[:], ln2_b[0:1, :].broadcast_to([P, D])).then_inc(s["ln2_in"], 16)
        for b in range(TB):
            sp.wait_ge(s["out_ready"], b + 1)
            sp.dma_start(out[0, b * P:(b + 1) * P, :], xres[:, b, :]).then_inc(s["stored"], 16)
        sp.wait_ge(s["stored"], 16 * TB)

    @block.gpsimd
    def _(pool):
        pool.memset(ident[:], 0.0).then_inc(s["pool_done"], 1)
        pool.wait_ge(s["pool_done"], 1)
        pool.affine_select(out=ident[:], in_=ident[:], compare_op=ALU.not_equal, fill=1.0, base=0,
                           pattern=[[-1, P]], channel_multiplier=1).then_inc(s["ident_ready"], 1)
        pool.wait_ge(s["ident_ready"], 1)
        pool.iota(iota[:], [[1, P]], base=0, channel_multiplier=0,
                  allow_small_or_imprecise_dtypes=True).then_inc(s["ident_ready"], 1)
        pool.wait_ge(s["ident_ready"], 2)
        pool.memset(eps, EPS).then_inc(s["ident_ready"], 1)
        pool.wait_ge(s["ident_ready"], 3)
        masks = ((WIN_W, GRID_W - 1 - WIN_W + WIN_W // 2, -1), (0, WIN_W // 2 - GRID_W, 1))
        done = 0
        for g, heads in enumerate(BIAS_HEADS):
            pool.wait_ge(s[f"rpb_in{g}"], 16 * ROWS * (heads[1] - heads[0]))
            for c0, base, sign in masks:
                for p0 in (0, GRID_W):
                    if done:
                        pool.wait_ge(s["mask_done"], done)
                    part = bias[p0:p0 + GRID_W, heads[0]:heads[1]] \
                        .rearrange("p h b (r c) -> p (h b r) c", c=GRID_W)[:, :, c0:c0 + GRID_W - WIN_W]
                    rows = (heads[1] - heads[0]) * TB * ROWS
                    pool.affine_select(out=part, in_=part, compare_op=ALU.is_ge, fill=MASKED, base=base,
                                       pattern=[[0, rows], [sign, GRID_W - WIN_W]],
                                       channel_multiplier=sign).then_inc(s["mask_done"], 1)
                    done += 1

    @block.scalar
    def _(act):
        def split_act(n, first_tp):
            for g in range(4):
                act.wait_ge(s["tp_done"], first_tp + g + 1)
                act.activation(act_hi[:, 2 * g:2 * g + 2, :].rearrange("p a b -> p (a b)"), ps[:, 4 + g, :],
                               ACT.Copy).then_inc(s["act_hi_done"], 1)

        split_act(0, 0)

        def copy_constants():
            act.wait_ge(s["tp_done"], 5)
            act.activation(wsT[:].rearrange("p a b -> p (a b)"), ps[:, 4, :], ACT.Copy).then_inc(s["tp_copied"], 1)
            act.wait_ge(s["tp_done"], 6)
            act.activation(skT[:].rearrange("p a b -> p (a b)"), ps[:, 5, 0:2 * P], ACT.Copy) \
                .then_inc(s["tp_copied"], 1)

        def free_acc(ins, j):
            ins.then_inc(s[f"acc_free{j % 2}"], 1)

        def evacuate(j):
            name = JOBS[j][0]
            a = acc(j)
            act.wait_ge(s["w_used"], LAST_HC[j] + 1)
            if name in ("q", "k", "v"):
                dst = {"q": qT, "k": kT, "v": v_sb}[name]
                free_acc(act.activation(dst[:].rearrange("p a b -> p (a b)"), a, ACT.Copy), j)
            elif name[0] == "g":
                i = j - JOB["ga0"]
                dst = gates[:, 4 * i:4 * i + 4, :].rearrange("p a b -> p (a b)")
                free_acc(act.activation(dst, a, ACT.Tanh, scale=0.5), j)
            elif name in ("sv", "su"):
                dst = sv_sb if name == "sv" else su_sb
                free_acc(act.activation(dst[:].rearrange("p a b -> p (a b)"), a, ACT.Gelu_apprx_tanh), j)
            elif name in ("w0", "w1", "w2", "w3"):
                i = int(name[1])
                if i >= 2:
                    act.wait_ge(s["key_scores"], i - 1)
                free_acc(act.activation(pqT[:, i % 2].rearrange("p a b -> p (a b)"), a, ACT.Copy), j)

        def attention_exp(h):
            act.wait_ge(s["max_done"], h + 1)
            for b in range(TB):
                act.activation(prob[:, h % 2, b, :], prob[:, h % 2, b, :], ACT.Exp,
                               bias=rmax[:, 2 * (h % 2) + b:2 * (h % 2) + b + 1],
                               accum_out=rsum[:, 2 * (h % 2) + b:2 * (h % 2) + b + 1]).then_inc(s["exp_done"], 1)

        def copy_probT(h):
            act.wait_ge(s["probT_done"], h + 1)
            if h >= 2:
                act.wait_ge(s["pv_done"], h - 1)
            act.activation(probT[:, h % 2].rearrange("p a b -> p (a b)"), ps[:, 5, :], ACT.Copy) \
                .then_inc(s["probT_copied"], 1)

        def yna_split(pair):
            act.wait_ge(s["pv_done"], 2 * pair + 2)
            act.activation(yna_hi[:, pair, :], ps[:, 6, 0:T], ACT.Copy).then_inc(s["yna_hi_done"], 1)

        def ysg_split(b):
            act.wait_ge(s["ysgT_done"], b + 1)
            act.activation(ysgT_hi[:, 2 * b:2 * b + 2, :].rearrange("p a b -> p (a b)"), ps[:, 7, :],
                           ACT.Copy).then_inc(s["ysgT_hi_done"], 1)

        def sqrt_var(n, cols):
            act.wait_ge(s["ln_var"], TB * (n + 1))
            act.activation(rstd[:, 0:cols], mv.rearrange("p (b s) -> p b s", s=2)[:, 0:cols, 1], ACT.Sqrt,
                           bias=eps).then_inc(s["ln_std"], 1)

        def copy_scores(i):
            act.wait_ge(s["key_scores"], i + 1)
            act.activation(sc[:, 2 * i:2 * i + 2].rearrange("p a b c d -> p (a b c d)"),
                           ps[:, 4:6, :].rearrange("p a b -> p (a b)"), ACT.Copy).then_inc(s["sc_copied"], 1)

        def round_uT(n, banks, dst):
            act.wait_ge(s["u_read"], n + 1)
            act.activation(dst.rearrange("p a b -> p (a b)"), ps[:, banks:banks + 2, :].rearrange("p a b -> p (a b)"),
                           ACT.Copy).then_inc(s["uT_hi_done"], 1)

        def pre_slot(k):
            return uT3_hi[:] if k % 3 == 2 else uT_hi[:, k % 3]

        for hc in range(NHC + 2):
            if hc < NHC:
                c = hc // 2
                if hc == 0:
                    act.wait_ge(s["w_first"], 16)
                else:
                    act.wait_ge(s[f"w_in{c % 2}"], 16 * (c // 2 + 1))
                if hc >= 2:
                    act.wait_ge(s["w_used"], hc - 1)
                act.activation(w_hi[:, hc % 2], half_source(hc), ACT.Copy).then_inc(s["w_hi_done"], 1)
            for j in range(len(JOBS)):
                if LAST_HC[j] == hc - 1 and not JOBS[j][0].startswith(("na", "sg", "o")):
                    evacuate(j)
            if hc == 3:
                copy_constants()
            h = hc - ATT0 - 1
            if 0 <= h < HEADS:
                attention_exp(h)
            if 0 <= h - 2 < HEADS:
                copy_probT(h - 2)
            if h - 4 >= 1 and (h - 4) % 2 == 1 and h - 4 < HEADS:
                yna_split((h - 4) // 2)
            if hc == HC["sv"] + 2:
                sqrt_var(0, TB)
            for b in range(2):
                if hc == YSGT0 + 2 * b + 1:
                    ysg_split(b)
            if hc in (HC["na"] + 2, HC["na"] + 3):
                i = hc - HC["na"] - 2
                act.wait_ge(s["merged_sum"], i + 1)
                act.activation(mrg_hi[:, 4 * i:4 * i + 4, :].rearrange("p a b -> p (a b)"),
                               gates[:, 4 * i:4 * i + 4, :].rearrange("p a b -> p (a b)"), ACT.Copy,
                               scale=0.5).then_inc(s["mrg_hi_done"], 1)
            if hc == NHC - 1:
                round_uT(0, 6, pre_slot(0))
                round_uT(1, 2, pre_slot(1))
            if hc == HC["w0"]:
                sqrt_var(1, TB)
                split_act(1, 6)
            if HC["w0"] + 3 <= hc and (hc - HC["w0"] - 3) % 2 == 0 and (hc - HC["w0"] - 3) // 2 < 4:
                copy_scores((hc - HC["w0"] - 3) // 2)
        def pre_six(i, last):
            for k in range(6):
                if not (last and k == 5):
                    round_uT(6 * i + k + 2, 6 - 4 * (k % 2), pre_slot(k + 2))
                act.wait_ge(s["a_done"], 6 * i + k + 1)
                act.activation(G[:, bass.ds((6 * i + (NB - NPRE + k)) * T, T)], ps[:, k % 2, 0:T],
                               ACT.Gelu_apprx_tanh).then_inc(s["act_done"], 1)

        with act.Fori(0, NPRE // 6 - 1) as i:
            pre_six(i, False)
        act.wait_ge(s["soft_in"], 1)
        act.activation(gw[:].rearrange("p a b -> p (a b)"), gw[:].rearrange("p a b -> p (a b)"), ACT.Exp) \
            .then_inc(s["soft_exp"], 1)
        pre_six(NPRE // 6 - 1, True)
        act.wait_ge(s["routeT_done"], 1)
        for n, dst in enumerate((e1T, e2T, gT)):
            act.activation(dst[:], ps[:, 2 + n // 2, (n % 2) * T:(n % 2 + 1) * T], ACT.Copy) \
                .then_inc(s["routeT_copied"], 1)
        G3 = G[:].rearrange("p (e t) -> p e t", t=T)

        def during(part, i, slot):
            h = PB * part + 2 * i + slot
            n = NPRE + h
            todo = NB - NPRE - PB * part
            round_uT(n + 1, 6, uT_hi[:, 1 - slot])
            act.wait_ge(s["a_done"], n + 1)
            act.activation(early[:].rearrange("p a b -> p (a b)")[:, bass.ds((2 * i + slot) * T, T)],
                           ps[:, 4 + slot, 0:T], ACT.Gelu_apprx_tanh).then_inc(s["act_done"], 1)
            for q in range(2):
                act.wait_ge(s["g_bank"], 2 * h + q + 1)
                act.activation(G3[:, 0:todo, bass.ds(8 * h + 4 * q, 4)],
                               ps[:, 2 * slot + q, :].rearrange("p (t e) -> p e t", t=4)[:, 0:todo, :], ACT.Copy) \
                    .then_inc(s["g_copied"], 1)

        for part in range(PARTS):
            if part:
                act.wait_ge(s["settled_mult"], part)
            with act.Fori(0, PB // 2) as i:
                for slot in range(2):
                    during(part, i, slot)
            top = NB - NPRE - PB * part
            if part < PARTS - 1:
                act.wait_ge(s["act_done"], NPRE + PB * (part + 1))
                act.activation(G3[:, top - PB:top, PT * (part + 1):T], early[:, :, PT * (part + 1):T], ACT.Copy) \
                    .then_inc(s["settled_copy"], 1)
                act.wait_ge(s["settled_copy"], part + 1)

        def round_v(slot, landed, place):
            act.wait_ge(s[f"v_in{place % 4}"], landed)
            for d in range(2):
                act.activation(v_hi[:, slot, d * 512:(d + 1) * 512], v_slot(place)[:, d * 512:(d + 1) * 512],
                               ACT.Copy).then_inc(s["v_hi_done"], 1)

        def round_turned(n, slot):
            act.wait_ge(s["u_turned"], n - NEARLY)
            act.activation(uT_hi[:, slot].rearrange("p a b -> p (a b)"),
                           uT_raw[:, slot].rearrange("p a b -> p (a b)"), ACT.Copy).then_inc(s["uT_hi_done"], 1)

        for slot in range(2):
            act.wait_ge(s["settled_mult"], PARTS + slot)
            round_v(slot, 16, slot)
        round_turned(NEARLY + 1, 1)
        with act.Fori(0, (NEARLY - 2) // BODY) as i:
            for k in range(BODY):
                act.wait_ge(s["y_done"], BODY * i + (k + 1))
                round_v(k % 2, 4 * BODY * i + 16 * ((2 + k) // 4 + 1), 2 + k)
        act.wait_ge(s["y_done"], NEARLY - 1)
        round_v(0, V_BEFORE + 16, 0)

        def pair(i, head, tail):
            for slot in range(2):
                n = 2 * i + slot
                act.wait_ge(s["a_done"], n + 1)
                if not head:
                    act.wait_ge(s["hid_done"], n - 1)
                act.activation(act_e[:, slot, :], ps[:, 4 + slot, 0:T], ACT.Gelu_apprx_tanh) \
                    .then_inc(s["act_done"], 1)
                if not tail:
                    round_turned(n + 2, slot)
                if tail and slot == 1:
                    continue
                act.wait_ge(s["y_done"], n)
                round_v(1 - slot, 16 * i + (V_BEFORE - 8 * NEARLY + 16 * (1 + slot)), 1 - slot)

        pair(NEARLY // 2, True, False)
        with act.Fori(NEARLY // 2 + 1, NB // 2 - 1) as i:
            pair(i, False, False)
        pair(NB // 2 - 1, False, True)
        sqrt_var(2, TB)

    @block.vector
    def _(dve):
        ch = Chain(dve, s["dve"])

        def split_act(first_tp, first_hi):
            for g in range(4):
                dve.wait_ge(s["act_hi_done"], first_hi + g + 1)
                dst = act_lo[:, 2 * g:2 * g + 2, :].rearrange("p a b -> p (a b)")
                hi = act_hi[:, 2 * g:2 * g + 2, :].rearrange("p a b -> p (a b)").bitcast(F32)
                dve.tensor_tensor(dst, ps[:, 4 + g, :], hi, ALU.subtract).then_inc(s["act_lo_done"], 1)

        def row_stats(src, t, q):
            ch.step(dve.bn_stats(stats[:, 12 * t + 6 * q:12 * t + 6 * q + 6], src[:, t, 512 * q:512 * q + 512]))

        def means_and_variances(parts):
            ch.wait()
            for t in range(TB):
                dve.bn_aggr(mv[:, 2 * t:2 * t + 2], stats[:, 12 * t:12 * t + 6 * parts]).then_inc(s["ln_var"], 1)

        def normed(n, src, g, b, dst, done, gb_in):
            dve.wait_ge(gb_in, 32)
            dve.wait_ge(s["ln_var"], TB * (n + 1))
            for t in range(TB):
                ch.step(dve.scalar_tensor_tensor(dst[:, t, :], src[:, t, :], mv[:, 2 * t:2 * t + 1], g[:],
                                                 ALU.subtract, ALU.mult))
                if t == 0:
                    dve.wait_ge(s["ln_std"], n + 1)
                    ch.step(dve.reciprocal(rstd[:, 0:TB], rstd[:, 0:TB]))
                ch.wait()
                dve.scalar_tensor_tensor(dst[:, t, :], dst[:, t, :], rstd[:, t:t + 1], b[:],
                                         ALU.mult, ALU.add).then_inc(done, 1)

        split_act(0, 0)

        def logits(h):
            dve.wait_ge(s["score_done"], h + 1)
            dve.wait_ge(s["mask_done"], 4 * (1 + [g for g, r in enumerate(BIAS_HEADS) if r[0] <= h < r[1]][0]))
            if h >= 2:
                dve.wait_ge(s["probT_done"], h - 1)
            dve.scalar_tensor_tensor(prob[:, h % 2], ps[:, 4, :].rearrange("p (b k) -> p b k", b=TB), DH ** -0.5,
                                     free(bias[:, h, 0, :], (T, TB), (-1, T), start=T - 1),
                                     ALU.mult, ALU.add).then_inc(s["logit_done"], 1)
            dve.wait_ge(s["logit_done"], h + 1)
            m = rmax[:, 2 * (h % 2):2 * (h % 2) + 2]
            ch.step(dve.tensor_reduce(m, prob[:, h % 2], AX_X, ALU.max))
            ch.wait()
            dve.tensor_scalar(m, m, -1.0, None, ALU.mult).then_inc(s["max_done"], 1)

        def normalise(h):
            dve.wait_ge(s["exp_done"], 2 * h + 2)
            r = rinv[:, 2 * (h % 2):2 * (h % 2) + 2]
            ch.step(dve.reciprocal(r, rsum[:, 2 * (h % 2):2 * (h % 2) + 2]))
            ch.wait()
            for b in range(TB):
                dve.tensor_scalar(prob[:, h % 2, b, :], prob[:, h % 2, b, :], r[:, b:b + 1], None,
                                  ALU.mult).then_inc(s["prob_ready"], 1)

        def yna_split(pair):
            dve.wait_ge(s["yna_hi_done"], pair + 1)
            dve.tensor_tensor(yna_lo[:, pair, :], ps[:, 6, 0:T], yna_hi[:, pair, :].bitcast(F32),
                              ALU.subtract).then_inc(s["yna_lo_done"], 1)

        def gate_spatial(b):
            dve.wait_ge(s["bs_in"], 16)
            dve.wait_ge(s["acc_free%d" % (JOB["su"] % 2)], JOB["su"] // 2 + 1)
            dve.wait_ge(s["mix_done"], b + 1)
            for g in range(GROUPS):
                dve.scalar_tensor_tensor(ysg[:, b, g * P:(g + 1) * P], ps[:, 7, g * P:(g + 1) * P],
                                         bsT[:, g:g + 1], su_sb[:, b, g * P:(g + 1) * P],
                                         ALU.add, ALU.mult).then_inc(s["ysg_done"], 1)

        def ysg_split(b):
            dve.wait_ge(s["ysgT_hi_done"], b + 1)
            hi = ysgT_hi[:, 2 * b:2 * b + 2, :].rearrange("p a b -> p (a b)").bitcast(F32)
            dve.tensor_tensor(ysgT_lo[:, 2 * b:2 * b + 2, :].rearrange("p a b -> p (a b)"),
                              ps[:, 7, :], hi, ALU.subtract).then_inc(s["ysgT_lo_done"], 1)

        def merge(j):
            name = JOBS[j][0]
            dve.wait_ge(s["w_used"], LAST_HC[j] + 1)
            i = int(name[-1])
            ga = gates[:, 4 * i:4 * i + 4, :].rearrange("p a b -> p (a b)")
            gb = gates[:, 8 + 4 * i:12 + 4 * i, :].rearrange("p a b -> p (a b)")
            if name[:2] == "sg":
                dve.wait_ge(s[f"acc_free{(JOB['gb1']) % 2}"], JOB["gb1"] // 2 + 1)
                dve.wait_ge(s[f"acc_free{(JOB['gb0']) % 2}"], JOB["gb0"] // 2 + 1)
                dve.scalar_tensor_tensor(gb, gb, 1.0, acc(j), ALU.add, ALU.mult) \
                    .then_inc(s[f"acc_free{j % 2}"], 1)
            else:
                dve.scalar_tensor_tensor(ga, ga, 1.0, acc(j), ALU.add, ALU.mult) \
                    .then_inc(s[f"acc_free{j % 2}"], 1)
                dve.wait_ge(s[f"acc_free{j % 2}"], j // 2 + 1)
                dve.tensor_tensor(ga, ga, gb, ALU.add).then_inc(s["merged_sum"], 1)

        def rest_merged(i):
            dve.wait_ge(s["mrg_hi_done"], i + 1)
            hi = mrg_hi[:, 4 * i:4 * i + 4, :].rearrange("p a b -> p (a b)").bitcast(F32)
            dve.scalar_tensor_tensor(mrg_lo[:, 4 * i:4 * i + 4, :].rearrange("p a b -> p (a b)"),
                                     gates[:, 4 * i:4 * i + 4, :].rearrange("p a b -> p (a b)"), 0.5, hi,
                                     ALU.mult, ALU.subtract).then_inc(s["mrg_lo_done"], 1)

        def residual(i):
            j = JOB["o0"] + i
            for t in range(TB):
                if i == 1 and t == 0:
                    dve.wait_ge(s["o1_first"], 1)
                else:
                    dve.wait_ge(s["w_used"], LAST_HC[j] + 1)
                cols = xres[:, t, i * W5:(i + 1) * W5]
                ins = dve.scalar_tensor_tensor(cols, cols, ALPHA, acc(j)[:, t * W5:(t + 1) * W5], ALU.mult, ALU.add)
                if t == 0:
                    ins.then_inc(s["residual"], 1)
                    dve.wait_ge(s["residual"], i + 1)
                else:
                    ins.then_inc(s[f"acc_free{j % 2}"], 1)
                    dve.wait_ge(s[f"acc_free{j % 2}"], j // 2 + 1)
                row_stats(xres, t, i)

        def top16(vals, idx, src, spare):
            ch.step(dve.max(vals[:, 0:8], src))
            ch.wait()
            ch.step(dve.max_index(idx[:, 0:8], vals[:, 0:8], src))
            ch.step(dve.match_replace(spare, vals[:, 0:8], src, LOWEST))
            ch.wait()
            ch.step(dve.max(vals[:, 8:16], spare))
            ch.wait()
            ch.step(dve.max_index(idx[:, 8:16], vals[:, 8:16], spare))

        def pick(n):
            h, t, f = n // 6, n // 3 % TB, n % 3
            dve.wait_ge(s["sc_copied"], h // 2 + 1)
            if f < 2:
                top16(topv[:, t, h, f, :], topi[:, t, h, f, :], sc[:, h, t, f, :], sc2[:])
            else:
                ch.wait()
                c = cand[:, t, :]
                a = free(topv[:, t, h, 0, :], (1, TOPK), (0, TOPK))
                b = free(topv[:, t, h, 1, :], (0, TOPK), (1, TOPK))
                ch.step(dve.tensor_tensor(c.rearrange("p (a b) -> p a b", a=TOPK), a, b, ALU.add))
                ch.wait()
                top16(cv[:, t, h, :], cpos[:, t, h, :], c, cand2[:])

        def pre_slots(k):
            return (uT3_hi[:], uT3_lo[:]) if k % 3 == 2 else (uT_hi[:, k % 3], uT_lo[:, k % 3])

        def rest_uT(n, banks, hi, lo):
            dve.wait_ge(s["uT_hi_done"], n + 1)
            dve.tensor_tensor(lo.rearrange("p a b -> p (a b)"), ps[:, banks:banks + 2, :].rearrange("p a b -> p (a b)"),
                              hi.rearrange("p a b -> p (a b)").bitcast(F32), ALU.subtract) \
                .then_inc(s["uT_lo_done"], 1)

        def pre_split(step):
            for n in range(2 + step * (NPRE - 1) // STEPS, 2 + (step + 1) * (NPRE - 1) // STEPS):
                rest_uT(n, 6 - 4 * (n % 2), *pre_slots(n))

        for hc in range(NHC + 2):
            if hc < NHC:
                dve.wait_ge(s["w_hi_done"], hc + 1)
                dve.tensor_tensor(w_lo[:, hc % 2], half_source(hc), w_hi[:, hc % 2].bitcast(F32),
                                  ALU.subtract).then_inc(s["w_lo_done"], 1)
            if hc in (HC["na"] + 2, HC["na"] + 3):
                rest_merged(hc - HC["na"] - 2)
            for j in range(len(JOBS)):
                if LAST_HC[j] == hc - 1:
                    if JOBS[j][0].startswith(("na", "sg")):
                        merge(j)
                    elif JOBS[j][0].startswith("o"):
                        residual(j - JOB["o0"])
            h = hc - ATT0 - 1
            if 0 <= h < HEADS:
                logits(h)
            if 0 <= h - 1 < HEADS:
                normalise(h - 1)
            if h - 4 >= 1 and (h - 4) % 2 == 1 and h - 4 < HEADS:
                yna_split((h - 4) // 2)
            if hc == HC["sv"] + 2:
                dve.wait_ge(s["acc_free%d" % (JOB["sv"] % 2)], JOB["sv"] // 2 + 1)
                for t in range(TB):
                    row_stats(sv_sb, t, 0)
                means_and_variances(1)
            if hc == HC["sv"] + 3:
                normed(0, sv_sb, sgn_g, sgn_b, sv_sb, s["sgln_done"], s["sgn_in"])
            for b in range(2):
                if hc == MIX0 + b + 1:
                    gate_spatial(b)
                if hc == YSGT0 + 2 * b + 1:
                    ysg_split(b)
            if hc == HC["w0"]:
                means_and_variances(2)
                normed(1, xres, ln1g, ln1b, xres, s["x1_ready"], s["ln1_in"])
                split_act(6, 4)
            if hc == NHC - 1:
                for n in range(2):
                    rest_uT(n, 6 - 4 * n, *pre_slots(n))
            if hc in PICKS_AT:
                for n in PICKS_AT[hc]:
                    pick(n)
        for n in range(PICKED, 6 * PH):
            pick(n)
            pre_split(n - PICKED)
        ch.wait()
        cvr = cv[:].rearrange("p t h k -> p (t h) k")
        gwr = gw[:].rearrange("p t (h k) -> p (t h) k", k=TOPK)
        dve.tensor_tensor(gwr, cvr, free(cv[:, 0, 0, :], (TOPK, TB * PH), (0, TOPK)), ALU.subtract) \
            .then_inc(s["soft_in"], 1)
        flat = cpos[:].rearrange("p t h k -> p (t h k)")
        ch.step(dve.tensor_scalar(chalf[:, 0].rearrange("p t h k -> p (t h k)"), flat, 4, None,
                                  ALU.logical_shift_right))
        ch.step(dve.tensor_scalar(chalf[:, 1].rearrange("p t h k -> p (t h k)"), flat, TOPK - 1, None,
                                  ALU.bitwise_and))
        ch.step(dve.tensor_copy(topf[:].rearrange("p t h f k -> p (t h f k)"),
                                topi[:].rearrange("p t h f k -> p (t h f k)")))
        ch.wait()
        ch.step(dve.tensor_copy(chalff[:].rearrange("p f t h k -> p (f t h k)"),
                                chalf[:].rearrange("p f t h k -> p (f t h k)")))
        ch.wait()
        step = 6 * PH - PICKED
        for t in range(TB):
            for f, dst in enumerate((e1f, e2f)):
                e = eq[:].rearrange("p (h j) a -> p h j a", h=PH)
                rank = free(chalff[:, f, t, 0, :], (1, SLOTS), (0, TOPK))
                ch.wait()
                ch.step(dve.tensor_tensor(eq[:], rank, free(iota[:, 0:1], (0, SLOTS), (1, TOPK)), ALU.is_equal))
                keys = free(topf[:, t, 0, f, :], (2 * TOPK, PH), (0, TOPK), (1, TOPK))
                pre_split(step)
                ch.wait()
                ch.step(dve.tensor_tensor(e, e, keys, ALU.mult))
                pre_split(step + 1)
                ch.wait()
                ch.step(dve.tensor_reduce(dst[:, t, :], eq[:], AX_X, ALU.add))
                pre_split(step + 2)
                step += 3
        dve.wait_ge(s["soft_exp"], 1)
        ch.step(dve.tensor_reduce(gsum, gwr, AX_X, ALU.add))
        ch.wait()
        ch.step(dve.reciprocal(ginv, gsum))
        ch.wait()
        dve.tensor_tensor(gwr, gwr, free(ginv, (1, TB * PH), (0, TOPK)), ALU.mult) \
            .then_inc(s["route_done"], 1)

        dve.wait_ge(s["routeT_copied"], 3)
        G3 = G[:].rearrange("p (e t) -> p e t", t=T)

        def scale_four(group, bank, part):
            dve.wait_ge(s["g_copied"], group + 1)
            first = NB - NPRE - PB * part
            cells = G3[:, first:NB, bass.ds(4 * group, 4)]
            dve.tensor_tensor(cells, ps[:, bank, :].rearrange("p (t e) -> p e t", t=4)[:, first:NB, :], cells,
                              ALU.mult).then_inc(s["g_scaled"], 1)

        def onehots_four(group, q, first):
            if not first:
                dve.wait_ge(s["g_bank"], group - 1)
            dve.tensor_tensor(onehot2[:, 4 * q:4 * q + 4, :], free(iota[:, 0:1], (0, 4), (1, NK)),
                              e2T[:, bass.ds(4 * group, 4)].unsqueeze(2).broadcast_to([P, 4, NK]), ALU.is_equal)
            for k in range(4):
                ins = dve.tensor_scalar(onehot1g[:, 4 * q + k, :], iota[:], e1T[:, bass.ds(4 * group + k, 1)],
                                        gT[:, bass.ds(4 * group + k, 1)], ALU.is_equal, ALU.mult)
            ins.then_inc(s["onehots"], 1)

        def settle(part, b0, blocks):
            first = NB - NPRE - PB * (part + 1) + b0
            cells = G3[:, first:first + blocks, 0:PT * (part + 1)]
            dve.tensor_tensor(cells, cells, early[:, b0:b0 + blocks, 0:PT * (part + 1)], ALU.mult) \
                .then_inc(s["settled_mult"], 1)

        def during(part, i, slot, head):
            h = PB * part + 2 * i + slot
            begins = isinstance(i, int) and slot == 0
            for q in range(2):
                onehots_four(2 * h + q, q, head)
            if begins and part:
                dve.wait_ge(s["act_done"], NPRE + PB * part)
                dve.wait_ge(s["g_copied"], 2 * PB * part)
                settle(part - 1, 0, PB)
            rest_uT(NPRE + h + 1, 6, uT_hi[:, 1 - slot], uT_lo[:, 1 - slot])
            for q in range(2):
                if not head:
                    scale_four(2 * h + q - 2, 2 * (1 - slot) + q, part - 1 if begins else part)
            if begins and part:
                dve.wait_ge(s["settled_mult"], part)
                dve.wait_ge(s["settled_copy"], part)

        for part in range(PARTS):
            for slot in range(2):
                during(part, 0, slot, part == 0 and slot == 0)
            with dve.Fori(1, PB // 2) as i:
                for slot in range(2):
                    during(part, i, slot, False)
        for q in range(2):
            scale_four(T // 4 - 2 + q, 2 + q, PARTS - 1)

        def rest_v(n, slot, place):
            for d in range(2):
                dve.wait_ge(s["v_hi_done"], 2 * n + d + 1)
                dve.tensor_tensor(v_lo[:, slot, d * 512:(d + 1) * 512], v_slot(place)[:, d * 512:(d + 1) * 512],
                                  v_hi[:, slot, d * 512:(d + 1) * 512].bitcast(F32),
                                  ALU.subtract).then_inc(s["v_lo_done"], 1)

        def split_hidden(n, slot, hidden, head):
            if not head:
                dve.wait_ge(s["y_done"], n - 1)
            dve.tensor_copy(hid_hi[:, slot, :], hidden).then_inc(s["hid_h"], 1)
            dve.wait_ge(s["hid_h"], n + 1)
            dve.tensor_tensor(hid_lo[:, slot, :], hidden, hid_hi[:, slot, :].bitcast(F32),
                              ALU.subtract).then_inc(s["hid_done"], 1)

        def turn(landed, slot):
            dve.wait_ge(s[f"u_in{slot}"], landed)
            dve.transpose(uT_raw[:, slot].rearrange("p k (c i) -> p c k i", c=NQ),
                          u_raw[:, slot, :].rearrange("p (c j k) -> p c k j", c=NQ, k=KD)).then_inc(s["u_turned"], 1)

        def rest_turned(n, slot):
            dve.wait_ge(s["uT_hi_done"], n + 1)
            dve.tensor_tensor(uT_lo[:, slot].rearrange("p a b -> p (a b)"),
                              uT_raw[:, slot].rearrange("p a b -> p (a b)"),
                              uT_hi[:, slot].rearrange("p a b -> p (a b)").bitcast(F32), ALU.subtract) \
                .then_inc(s["uT_lo_done"], 1)

        dve.wait_ge(s["g_scaled"], T // 4)
        dve.wait_ge(s["act_done"], NEARLY)
        for slot in range(2):
            settle(PARTS - 1, slot * (PB // 2), PB // 2)
            split_hidden(slot, slot, G[:, (NB - NPRE + slot) * T:(NB - NPRE + slot + 1) * T], True)
            rest_v(slot, slot, slot)
        turn(16 * (NEARLY // 2 + NQ), 1)
        with dve.Fori(0, (NPRE - 2) // BODY) as i:
            for k in range(BODY):
                split_hidden(BODY * i + (2 + k), k % 2, G[:, bass.ds((BODY * i + (NB - NPRE + 2 + k)) * T, T)], False)
                rest_v(BODY * i + (2 + k), k % 2, 2 + k)
        rest_turned(NEARLY + 1, 1)
        dve.wait_ge(s["settled_mult"], PARTS + 1)
        with dve.Fori(0, NDUR // BODY) as i:
            for k in range(BODY):
                split_hidden(BODY * i + (NPRE + k), k % 2, G[:, bass.ds((BODY * i + (NB - NEARLY + k)) * T, T)], False)
                rest_v(BODY * i + (NPRE + k), k % 2, NPRE + k)

        def pair(j, tail):
            for slot in range(2):
                n = 2 * j + (NEARLY + slot)
                dve.wait_ge(s["act_done"], n + 1)
                dve.tensor_tensor(act_e[:, slot, :], act_e[:, slot, :], G[:, bass.ds((2 * j + slot) * T, T)], ALU.mult) \
                    .then_inc(s["hid_m"], 1)
                dve.wait_ge(s["hid_m"], n - NEARLY + 1)
                split_hidden(n, slot, act_e[:, slot, :], False)
                if not tail:
                    before = NEARLY // 2 + (1 if slot == 0 else 0)
                    turn(16 * NQ * j + (16 * before + 16 * NQ * (1 + slot)), slot)
                rest_v(n, slot, slot)
                if not tail:
                    rest_turned(n + 2, slot)

        with dve.Fori(0, (NB - NEARLY) // 2 - 1) as j:
            pair(j, False)
        pair((NB - NEARLY) // 2 - 1, True)
        for t in range(TB):
            dve.wait_ge(*((s["y_first"], 1), (s["y_done"], NB))[t])
            ch.step(dve.scalar_tensor_tensor(xres[:, t, :], xres[:, t, :], ALPHA,
                                             ps[:, 2 * t:2 * t + 2, :].rearrange("p a b -> p (a b)"),
                                             ALU.mult, ALU.add))
            ch.wait()
            for q in range(2):
                row_stats(xres, t, q)
        means_and_variances(2)
        normed(2, xres, ln2g, ln2b, xres, s["out_ready"], s["ln2_in"])

    @block.tensor
    def _(pe):
        pe.wait_ge(s["ident_ready"], 3)

        def columns(ap, k):
            return ap.rearrange("p (c k) -> p c k", k=KD)[:, :, k]

        def transpose_rows(ready, wait_free):
            for t, g in ((t, g) for t in range(TB) for g in range(4)):
                if g == 0:
                    if t == 0:
                        wait_free()
                    pe.wait_ge(*ready[t])
                for k in range(2):
                    ins = pe.transpose(ps[:, 4 + g, k * T + t * P:k * T + (t + 1) * P],
                                       columns(xres[:, t, :], 2 * g + k), ident[:])
                if t == TB - 1:
                    ins.then_inc(s["tp_done"], 1)

        transpose_rows(2 * [(s["x_in"], 16)], lambda: None)

        def transpose_constants():
            pe.wait_ge(s["act_lo_done"], 2)
            pe.wait_ge(s["ws_in"], 16)
            for g in range(GROUPS):
                ins = pe.transpose(ps[:, 4, g * P:(g + 1) * P], ws_raw[:, g, :], ident[:])
            ins.then_inc(s["tp_done"], 1)
            pe.wait_ge(s["sk_in"], 32)
            for f in range(2):
                ins = pe.transpose(ps[:, 5, f * P:(f + 1) * P], sk_raw[:, f, :], ident[:])
            ins.then_inc(s["tp_done"], 1)

        def scores(h):
            pe.wait_ge(s["acc_free1"], 1)
            if h == 0:
                pe.wait_ge(s["tp_copied"], 2)
            else:
                pe.wait_ge(s["logit_done"], h)
            p0 = DH * (h % 2)
            for b in range(TB):
                ins = pe.matmul(ps[:, 4, b * T:(b + 1) * T], qT[p0:p0 + DH, h // 2, b * P:(b + 1) * P],
                                kT[p0:p0 + DH, h // 2, :], start=True, stop=True)
            ins.then_inc(s["score_done"], 1)

        def transpose_probs(h):
            pe.wait_ge(s["prob_ready"], 2 * h + 2)
            if h >= 1:
                pe.wait_ge(s["probT_copied"], h)
            for kb in range(TB):
                for b in range(TB):
                    ins = pe.transpose(ps[:, 5, kb * T + b * P:kb * T + (b + 1) * P],
                                       prob[:, h % 2, b, kb * P:(kb + 1) * P], ident[:])
            ins.then_inc(s["probT_done"], 1)

        def times_v(h):
            pe.wait_ge(s["probT_copied"], h + 1)
            pe.wait_ge(s["acc_free0"], 2)
            if h >= 2 and h % 2 == 0:
                pe.wait_ge(s["yna_lo_done"], h // 2)
            p0 = DH * (h % 2)
            for kb in range(TB):
                ins = pe.matmul(ps[p0:p0 + DH, 6, 0:T], v_sb[:, kb, h * DH:(h + 1) * DH], probT[:, h % 2, kb, :],
                                start=(kb == 0), stop=(kb == TB - 1))
            ins.then_inc(s["pv_done"], 1)

        def mix(b):
            pe.wait_ge(s["sgln_done"], b + 1)
            if b:
                pe.wait_ge(s["ysg_done"], GROUPS)
            for g in range(GROUPS):
                ins = pe.matmul(ps[:, 7, g * P:(g + 1) * P], wsT[:, g, :], sv_sb[:, b, g * P:(g + 1) * P],
                                start=True, stop=True)
            ins.then_inc(s["mix_done"], 1)

        def transpose_ysg(b2):
            pe.wait_ge(s["ysg_done"], TB * GROUPS)
            if b2:
                pe.wait_ge(s["ysgT_lo_done"], 1)
            for k in range(2):
                for t in range(TB):
                    g = 2 * b2 + k
                    ins = pe.transpose(ps[:, 7, k * T + t * P:k * T + (t + 1) * P],
                                       ysg[:, t, g * P:(g + 1) * P], ident[:])
            ins.then_inc(s["ysgT_done"], 1)

        def key_scores(i):
            j = JOB["w0"] + i
            pe.wait_ge(s[f"acc_free{j % 2}"], j // 2 + 1)
            if i == 0:
                pe.wait_ge(s["act_lo_done"], 8)
            else:
                pe.wait_ge(s["sc_copied"], i)
            for hh in range(2):
                for t in range(TB):
                    for f in range(2):
                        c = (t * 2 + f) * NK
                        ins = pe.matmul(ps[:, 4 + hh, c:c + NK], pqT[:, i % 2, 2 * hh + f, t * P:(t + 1) * P],
                                        skT[:, f, :], start=True, stop=True)
            ins.then_inc(s["key_scores"], 1)

        def transpose_u(landed, slot, banks):
            pe.wait_ge(s[f"u_in{slot}"], landed)
            for k in range(KD):
                ins = pe.transpose(ps[:, banks + k // 4, (k % 4) * P:(k % 4 + 1) * P],
                                   columns(u_raw[:, slot, :], k), ident[:])
            ins.then_inc(s["u_read"], 1)

        for hc in range(NHC + 2):
            if hc == NHC - 1:
                pe.wait_ge(s["act_lo_done"], 8)
                transpose_u(16, 0, 6)
                pe.wait_ge(s[f"acc_free{JOB['w2'] % 2}"], JOB["w2"] // 2 + 1)
                transpose_u(16, 1, 2)
            if hc < NHC:
                j = JOB_OF_HC[hc]
                name, hcs = JOBS[j]
                first = hc == hcs[0]
                if first and j >= 2:
                    pe.wait_ge(s[f"acc_free{j % 2}"], j // 2)
                if name in ("na0", "sg0"):
                    n = {"na0": ("yna_lo_done", HEADS // 2), "sg0": ("ysgT_lo_done", 2)}[name]
                    pe.wait_ge(s[n[0]], n[1])
                if name == "o0" and first:
                    pe.wait_ge(s["mrg_lo_done"], 1)
                if name == "o0" and not first:
                    pe.wait_ge(s["mrg_lo_done"], 2)
                if name == "q":
                    pe.wait_ge(s["act_lo_done"], 2 if first else 4)
                if name == "w0":
                    pe.wait_ge(s["act_lo_done"], 6 if first else 8)
                pe.wait_ge(s["w_lo_done"], hc + 1)
                a_hi, a_lo = {"n": (yna_hi, yna_lo), "s": (act_hi, act_lo), "o": (mrg_hi, mrg_lo)} \
                    .get(name[0], (act_hi, act_lo))
                if name in ("sg0", "sg1"):
                    a_hi, a_lo = ysgT_hi, ysgT_lo
                k0 = KW * hcs.index(hc)
                natural = name in ("v", "sv", "su", "o0", "o1")
                a = acc(j)
                slot = hc % 2
                for m in range(TB if natural else 4):
                    for k in range(KW):
                        for part in range(3):
                            ah = (a_hi, a_lo, a_hi)[part]
                            wh = (w_hi, w_hi, w_lo)[part]
                            if natural:
                                dst = a[:, m * W5:(m + 1) * W5]
                                l = ah[:, k0 + k, m * P:(m + 1) * P]
                                r = wh[:, slot, k, :]
                                opens = first and k == 0 and part == 0
                            else:
                                dst = a[:, m * T:(m + 1) * T]
                                l = wh[:, slot, k, m * P:(m + 1) * P]
                                r = ah[:, k0 + k, :]
                                opens = first and k == 0 and part == 0 and m % 2 == 0
                            ins = pe.matmul(dst, l, r, start=opens, stop=(hc == hcs[-1] and k == KW - 1 and part == 2),
                                            skip_group_check=True)
                    if name == "o1" and hc == hcs[-1] and m == 0:
                        ins.then_inc(s["o1_first"], 1)
                ins.then_inc(s["w_used"], 1)
            if hc == 1:
                transpose_constants()
            h = hc - ATT0
            if 0 <= h < HEADS:
                scores(h)
            if 0 <= h - 2 < HEADS:
                transpose_probs(h - 2)
            if 0 <= h - 4 < HEADS:
                times_v(h - 4)
            for b in range(2):
                if hc == MIX0 + b:
                    mix(b)
                if hc == YSGT0 + 2 * b:
                    transpose_ysg(b)
            if hc == HC["o1"] + 1:
                def free_banks():
                    pe.wait_ge(s["ysgT_lo_done"], 2)
                    pe.wait_ge(s["yna_lo_done"], HEADS // 2)
                    pe.wait_ge(s["probT_copied"], HEADS)
                transpose_rows([(s["x1_ready"], t + 1) for t in range(TB)], free_banks)
            if hc >= HC["w0"] + 2 and (hc - HC["w0"] - 2) % 2 == 0 and (hc - HC["w0"] - 2) // 2 < 4:
                key_scores((hc - HC["w0"] - 2) // 2)

        def expert_inputs(hi, lo, bank):
            for k in range(KD):
                for part in range(3):
                    ins = pe.matmul(ps[:, bank, 0:T], (hi, hi, lo)[part][:, k, :],
                                    (act_hi, act_lo, act_hi)[part][:, k, :],
                                    start=(k == 0 and part == 0), stop=(k == KD - 1 and part == 2))
            ins.then_inc(s["a_done"], 1)

        def pre_slots(k):
            return (uT3_hi[:], uT3_lo[:]) if k % 3 == 2 else (uT_hi[:, k % 3], uT_lo[:, k % 3])

        def pre_six(i, head, last):
            for k in range(6):
                n = 6 * i + k
                pe.wait_ge(s["uT_lo_done"], n + 1)
                if not (last and k == 5):
                    transpose_u(48 * i + 16 * ((k + 2) // 2 + 1), k % 2, 6 - 4 * (k % 2))
                if not (head and k < 2):
                    pe.wait_ge(s["act_done"], n - 1)
                expert_inputs(*pre_slots(k), k % 2)

        pre_six(0, True, False)
        with pe.Fori(1, NPRE // 6 - 1) as i:
            pre_six(i, False, False)
        pre_six(NPRE // 6 - 1, False, True)
        pe.wait_ge(s["route_done"], 1)
        for n, src in enumerate((e1f, e2f, gw)):
            for t in range(TB):
                ins = pe.transpose(ps[:, 2 + n // 2, (n % 2) * T + t * P:(n % 2) * T + (t + 1) * P], src[:, t, :], ident[:])
        ins.then_inc(s["routeT_done"], 1)
        pe.wait_ge(s["uT_lo_done"], NPRE + 1)
        transpose_u(8 * NPRE + 16, 1, 6)
        expert_inputs(uT_hi[:, 0], uT_lo[:, 0], 4)

        def during(part, i, slot, head):
            h = PB * part + 2 * i + slot
            n = NPRE + h
            if not (head and slot == 0):
                pe.wait_ge(s["uT_lo_done"], n + 1)
                transpose_u(8 * (NPRE + PB * part) + 16 * i + 16 + 16 * slot, 1 - slot, 6)
                pe.wait_ge(s["act_done"], n - 1)
                expert_inputs(uT_hi[:, slot], uT_lo[:, slot], 4 + slot)
            for q in range(2):
                pe.wait_ge(s["onehots"], 2 * h + q + 1)
                if not head:
                    pe.wait_ge(s["g_copied"], 2 * h + q - 3)
                    pe.wait_ge(s["g_scaled"], 2 * h + q - 3)
                for k in range(4):
                    ins = pe.matmul(ps[:, 2 * slot + q, k * NK:(k + 1) * NK], onehot2[:, 4 * q + k, :],
                                    onehot1g[:, 4 * q + k, :], start=True, stop=True)
                ins.then_inc(s["g_bank"], 1)

        pe.wait_ge(s["act_done"], NPRE)
        pe.wait_ge(s["routeT_copied"], 3)
        for part in range(PARTS):
            if part == 0:
                for slot in range(2):
                    during(0, 0, slot, True)
            with pe.Fori(1 if part == 0 else 0, PB // 2) as i:
                for slot in range(2):
                    during(part, i, slot, False)

        def expert_outputs(slot, opens, closes):
            for t in range(TB):
                for part in range(3):
                    h = (hid_hi, hid_lo, hid_hi)[part][:, slot, t * P:(t + 1) * P]
                    v = (v_hi, v_hi, v_lo)[part]
                    for d in range(2):
                        ins = pe.matmul(ps[:, 2 * t + d, :], h, v[:, slot, d * 512:(d + 1) * 512],
                                        start=(opens and part == 0), stop=(closes and part == 2),
                                        skip_group_check=True)
                if closes and t == 0:
                    ins.then_inc(s["y_first"], 1)
            ins.then_inc(s["y_done"], 1)

        pe.wait_ge(s["uT_lo_done"], NEARLY + 1)
        pe.wait_ge(s["act_done"], NEARLY - 1)
        expert_inputs(uT_hi[:, 0], uT_lo[:, 0], 4)
        pe.wait_ge(s["g_copied"], T // 4)
        pe.wait_ge(s["g_scaled"], T // 4)

        def outputs_of(n, slot, opens, closes):
            pe.wait_ge(s["hid_done"], n + 1)
            pe.wait_ge(s["v_lo_done"], 2 * n + 2)
            expert_outputs(slot, opens, closes)

        outputs_of(0, 0, True, False)
        outputs_of(1, 1, False, False)
        with pe.Fori(0, (NEARLY - 2) // BODY) as i:
            for k in range(BODY):
                outputs_of(BODY * i + (2 + k), k % 2, False, False)

        def pair(i, head):
            for slot in range(2):
                n = 2 * i + slot
                if not (head and slot == 0):
                    pe.wait_ge(s["uT_lo_done"], n + 1)
                    pe.wait_ge(s["act_done"], n - 1)
                    expert_inputs(uT_hi[:, slot], uT_lo[:, slot], 4 + slot)
                if not (head and slot == 0):
                    outputs_of(n - 1, 1 - slot, False, False)

        pair(NEARLY // 2, True)
        with pe.Fori(NEARLY // 2 + 1, NB // 2) as i:
            pair(i, False)
        outputs_of(NB - 1, 1, False, True)

    blocks.__exit__(None, None, None)


_INS = ["x", "w_in", "na_rpb", "sg_norm_g", "sg_norm_b", "sg_spatial_w", "sg_spatial_b", "w_branch_na",
        "w_branch_sg", "w_out", "ln1_g", "ln1_b", "peer_wq", "peer_subkeys1", "peer_subkeys2", "peer_u",
        "peer_v", "ln2_g", "ln2_b"]
_OUTS = [((1, T, D), "float32")]


def kernel(**inputs):
    import numpy as _np
    import concourse.bacc as _bacc
    from concourse import mybir as _mybir
    from concourse.bass_utils import run_bass_kernel_spmd as _run

    nc = _bacc.Bacc("TRN2", target_bir_lowering=False, num_devices=1)
    arrays, args = {}, []
    for name in _INS:
        a = inputs[name]
        if name == "na_rpb":
            a = _np.asarray(a)[:, :, ::-1, ::-1]
        a = _np.ascontiguousarray(a)
        arrays[f"in_{name}_dram"] = a
        args.append(nc.dram_tensor(f"in_{name}_dram", a.shape, _mybir.dt.from_np(a.dtype), kind="ExternalInput").ap())
    for i, (shape, dtype) in enumerate(_OUTS):
        dt = _mybir.dt.from_np(_np.dtype(dtype))
        args.append(nc.dram_tensor(f"out_{i}_dram", shape, dt, kind="ExternalOutput").ap())
    hybrid_block(nc, *args)
    r = _run(nc, [arrays], core_ids=[0])
    got = tuple(r.results[0][f"out_{i}_dram"] for i in range(len(_OUTS)))
    return got[0]
```
